# Optimizing a Trainium2 kernel written in Bass

```python
import jax, jax.numpy as jnp
from jax import lax
import numpy as np

D_MODEL = 1024
BATCH = 1
SEQ = 256
DEPTH = 2

N_A = DEPTH // 2
N_B = DEPTH - N_A
HEAD_DIM = 64
N_MIX_HEADS = 12
N_KV_GROUPS = 2
HEADS_PER_GROUP = N_MIX_HEADS // N_KV_GROUPS
N_MEM_HEADS = 4
N_MEM = 256
L_CMP = 32
CMP_STRIDE = 16
CMP_HIDDEN = 256
L_SEL = 64
TOP_N = 16
WINDOW = 512
Q_BLOCK = 128
D_FF = 2816
CONV_WIDTH = 3
ROPE_THETA = 10000.0
EPS = 1e-6
NEG = -1e30
FORCE_BONUS = 1e4

MIX_W = N_MIX_HEADS * HEAD_DIM
MEM_W = N_MEM_HEADS * HEAD_DIM
BRANCH_KV_W = 6 * N_KV_GROUPS * HEAD_DIM
GATE_W = 3 * N_MIX_HEADS
A_IN = MIX_W + BRANCH_KV_W + GATE_W + MEM_W
B_IN = MIX_W + MEM_W
SHARED_W = 2 * MIX_W + N_MIX_HEADS


def rms_norm(x, g):
    xf = x.astype(jnp.float32)
    y = xf * lax.rsqrt(jnp.mean(xf * xf, axis=-1, keepdims=True) + EPS)
    return (y * g.astype(jnp.float32)).astype(x.dtype)

def rope(x, pos):
    half = HEAD_DIM // 2
    inv = ROPE_THETA ** (-jnp.arange(half, dtype=jnp.float32) / half)
    ang = pos.astype(jnp.float32)[:, None] * inv[None, :]
    shape = (1, pos.shape[0]) + (1,) * (x.ndim - 3) + (half,)
    cos = jnp.cos(ang).reshape(shape)
    sin = jnp.sin(ang).reshape(shape)
    xf = x.astype(jnp.float32)
    x1, x2 = xf[..., :half], xf[..., half:]
    return jnp.concatenate([x1 * cos - x2 * sin, x2 * cos + x1 * sin], axis=-1).astype(x.dtype)

def masked_softmax(s, mask):
    s = jnp.where(mask, s, NEG)
    s = s - jnp.max(s, axis=-1, keepdims=True)
    e = jnp.exp(s) * mask
    return e / jnp.maximum(jnp.sum(e, axis=-1, keepdims=True), 1e-30)

def compress_blocks(u, pos_emb, w1, b1, w2, b2):
    B, S, G, dh = u.shape
    n_cmp = (S - L_CMP) // CMP_STRIDE + 1
    idx = jnp.arange(n_cmp)[:, None] * CMP_STRIDE + jnp.arange(L_CMP)[None, :]
    blocks = u[:, idx] + pos_emb[:, None, :]
    flat = blocks.transpose(0, 1, 3, 2, 4).reshape(B, n_cmp, G, L_CMP * dh)
    return jax.nn.gelu(flat @ w1 + b1) @ w2 + b2

def nsa_attention(q, kc, vc, k_slc, v_slc, k_win, v_win, gates):
    B, S, G, HG, dh = q.shape
    n_cmp = kc.shape[1]
    n_sel = S // L_SEL
    n_top = min(TOP_N, n_sel)
    n_qb = S // Q_BLOCK
    scale = HEAD_DIM ** -0.5
    cmp_start = jnp.arange(n_cmp) * CMP_STRIDE
    cmp_end = cmp_start + L_CMP - 1
    sel_start = jnp.arange(n_sel) * L_SEL
    overlap = ((cmp_start[:, None] < sel_start[None, :] + L_SEL)
               & (cmp_start[:, None] + L_CMP > sel_start[None, :])).astype(jnp.float32)
    kb = k_slc.reshape(B, n_sel, L_SEL, G, dh).transpose(0, 3, 1, 2, 4)
    vb = v_slc.reshape(B, n_sel, L_SEL, G, dh).transpose(0, 3, 1, 2, 4)
    kw_pad = jnp.pad(k_win, ((0, 0), (WINDOW, 0), (0, 0), (0, 0)))
    vw_pad = jnp.pad(v_win, ((0, 0), (WINDOW, 0), (0, 0), (0, 0)))
    bi = jnp.arange(B)[:, None, None, None]
    gi = jnp.arange(G)[None, :, None, None]
    j_sel = jnp.arange(n_sel)

    def block(args):
        c, qc, gc = args
        t = c * Q_BLOCK + jnp.arange(Q_BLOCK)
        s = jnp.einsum('btghd,bngd->bghtn', qc, kc).astype(jnp.float32) * scale
        p_cmp = masked_softmax(s, cmp_end[None, :] <= t[:, None])
        o_cmp = jnp.einsum('bghtn,bngd->btghd', p_cmp.astype(vc.dtype), vc)
        imp = jnp.einsum('bghtn,nj->bgtj', p_cmp, overlap)
        blk_t = t // L_SEL
        forced = (j_sel[None, :] == 0) | (j_sel[None, :] == blk_t[:, None]) | (j_sel[None, :] == blk_t[:, None] - 1)
        valid = j_sel[None, :] <= blk_t[:, None]
        score = jnp.where(valid, imp + FORCE_BONUS * forced.astype(jnp.float32), NEG)
        _, idx = lax.top_k(score, n_top)
        kg = kb[bi, gi, idx]
        vg = vb[bi, gi, idx]
        key_pos = idx[..., None] * L_SEL + jnp.arange(L_SEL)
        m_sel = (key_pos <= t[None, None, :, None, None]).reshape(B, G, 1, Q_BLOCK, n_top * L_SEL)
        s = jnp.einsum('btghd,bgtnld->bghtnl', qc, kg).astype(jnp.float32) * scale
        p = masked_softmax(s.reshape(B, G, HG, Q_BLOCK, n_top * L_SEL), m_sel)
        o_slc = jnp.einsum('bghtk,bgtkd->btghd', p.astype(vg.dtype),
                           vg.reshape(B, G, Q_BLOCK, n_top * L_SEL, dh))
        kw = lax.dynamic_slice_in_dim(kw_pad, c * Q_BLOCK, WINDOW + Q_BLOCK, axis=1)
        vw = lax.dynamic_slice_in_dim(vw_pad, c * Q_BLOCK, WINDOW + Q_BLOCK, axis=1)
        s_pos = c * Q_BLOCK - WINDOW + jnp.arange(WINDOW + Q_BLOCK)
        m_win = (s_pos[None, :] >= 0) & (s_pos[None, :] <= t[:, None]) & (t[:, None] - s_pos[None, :] < WINDOW)
        s = jnp.einsum('btghd,bsgd->bghts', qc, kw).astype(jnp.float32) * scale
        p = masked_softmax(s, m_win)
        o_win = jnp.einsum('bghts,bsgd->btghd', p.astype(vw.dtype), vw)
        g = gc.reshape(B, Q_BLOCK, G, HG, 3)
        return g[..., 0:1] * o_cmp + g[..., 1:2] * o_slc + g[..., 2:3] * o_win

    q_chunks = jnp.moveaxis(q.reshape(B, n_qb, Q_BLOCK, G, HG, dh), 1, 0)
    g_chunks = jnp.moveaxis(gates.reshape(B, n_qb, Q_BLOCK, N_MIX_HEADS, 3), 1, 0)
    out = lax.map(block, (jnp.arange(n_qb), q_chunks, g_chunks))
    return jnp.moveaxis(out, 0, 1).reshape(B, S, MIX_W)

def nsa_mixer(h, w_in, gate_b, cmp_pos, cmp_w1, cmp_b1, cmp_w2, cmp_b2, pos):
    B, S, _ = h.shape
    proj = h @ w_in
    q = proj[..., :MIX_W].reshape(B, S, N_MIX_HEADS, HEAD_DIM)
    kv = proj[..., MIX_W:MIX_W + BRANCH_KV_W].reshape(B, S, 6, N_KV_GROUPS, HEAD_DIM)
    gate_logit = proj[..., MIX_W + BRANCH_KV_W:MIX_W + BRANCH_KV_W + GATE_W]
    q_mem = proj[..., MIX_W + BRANCH_KV_W + GATE_W:].reshape(B, S, N_MEM_HEADS, HEAD_DIM)
    q = rope(q, pos).reshape(B, S, N_KV_GROUPS, HEADS_PER_GROUP, HEAD_DIM)
    k_cmp, v_cmp, k_slc, v_slc, k_win, v_win = (kv[:, :, i] for i in range(6))
    n_cmp = (S - L_CMP) // CMP_STRIDE + 1
    cmp_end = jnp.arange(n_cmp) * CMP_STRIDE + L_CMP - 1
    kc = rope(compress_blocks(k_cmp, cmp_pos[0], cmp_w1[0], cmp_b1[0], cmp_w2[0], cmp_b2[0]), cmp_end)
    vc = compress_blocks(v_cmp, cmp_pos[1], cmp_w1[1], cmp_b1[1], cmp_w2[1], cmp_b2[1])
    gates = jax.nn.sigmoid(gate_logit + gate_b).reshape(B, S, N_MIX_HEADS, 3)
    o = nsa_attention(q, kc, vc, rope(k_slc, pos), v_slc, rope(k_win, pos), v_win, gates)
    return o, q_mem

def forgetting_attention(q, k, v, dcum):
    B, S, H, dh = q.shape
    scale = HEAD_DIM ** -0.5
    outs = []
    for c in range(S // Q_BLOCK):
        lo, hi = c * Q_BLOCK, (c + 1) * Q_BLOCK
        t = lo + jnp.arange(Q_BLOCK)
        s = jnp.einsum('bthd,bshd->bhts', q[:, lo:hi], k[:, :hi]).astype(jnp.float32) * scale
        s = s + dcum[:, :, lo:hi, None] - dcum[:, :, None, :hi]
        p = masked_softmax(s, jnp.arange(hi)[None, :] <= t[:, None])
        outs.append(jnp.einsum('bhts,bshd->bthd', p.astype(v.dtype), v[:, :hi]))
    return jnp.concatenate(outs, axis=1).reshape(B, S, MIX_W)

def memory_attention(q_mem, mem, g_mem, w_mem_kv):
    B, M, _ = mem.shape
    kv = (rms_norm(mem, g_mem) @ w_mem_kv).reshape(B, M, 2, N_MEM_HEADS, HEAD_DIM)
    s = jnp.einsum('bthd,bmhd->bhtm', q_mem, kv[:, :, 0]).astype(jnp.float32) * HEAD_DIM ** -0.5
    p = jax.nn.softmax(s, axis=-1).astype(kv.dtype)
    o = jnp.einsum('bhtm,bmhd->bthd', p, kv[:, :, 1])
    return o.reshape(q_mem.shape[0], q_mem.shape[1], MEM_W)

def conv_ffn(h, w_up, conv_w, conv_b, w_down):
    u = h @ w_up
    C = u.shape[-1]
    u = lax.conv_general_dilated(u, conv_w[:, None, :], window_strides=(1,),
                                 padding=[(CONV_WIDTH - 1, 0)],
                                 dimension_numbers=('NWC', 'WIO', 'NWC'),
                                 feature_group_count=C) + conv_b
    a, b = u[..., :D_FF], u[..., D_FF:]
    return (jax.nn.silu(a) * b) @ w_down

def first_inputs(seed: int = 0) -> dict:
    key = jax.random.key(seed)
    ks = jax.random.split(key, 24)
    f32 = jnp.float32
    nrm = lambda k, shape, scale: jax.random.normal(k, shape, f32) * scale
    return {
        "x": nrm(ks[0], (BATCH, SEQ, D_MODEL), 1.0),
        "mem": nrm(ks[1], (BATCH, N_MEM, D_MODEL), 1.0),
        "attn_norm": 1.0 + nrm(ks[2], (DEPTH, D_MODEL), 0.02),
        "ffn_norm": 1.0 + nrm(ks[3], (DEPTH, D_MODEL), 0.02),
        "mem_norm": 1.0 + nrm(ks[4], (DEPTH, D_MODEL), 0.02),
        "w_mem_kv": nrm(ks[5], (DEPTH, D_MODEL, 2 * MEM_W), D_MODEL ** -0.5),
        "w_o": nrm(ks[6], (DEPTH, MIX_W + MEM_W, D_MODEL), (MIX_W + MEM_W) ** -0.5),
        "w_up": nrm(ks[7], (DEPTH, D_MODEL, 2 * D_FF), D_MODEL ** -0.5),
        "conv_w": nrm(ks[8], (DEPTH, CONV_WIDTH, 2 * D_FF), CONV_WIDTH ** -0.5),
        "conv_b": nrm(ks[9], (DEPTH, 2 * D_FF), 0.01),
        "w_down": nrm(ks[10], (DEPTH, D_FF, D_MODEL), D_FF ** -0.5),
        "a_w_in": nrm(ks[11], (N_A, D_MODEL, A_IN), D_MODEL ** -0.5),
        "a_gate_b": nrm(ks[12], (N_A, GATE_W), 0.01),
        "a_cmp_pos": nrm(ks[13], (N_A, 2, L_CMP, HEAD_DIM), 0.1),
        "a_cmp_w1": nrm(ks[14], (N_A, 2, L_CMP * HEAD_DIM, CMP_HIDDEN), (L_CMP * HEAD_DIM) ** -0.5),
        "a_cmp_b1": nrm(ks[15], (N_A, 2, CMP_HIDDEN), 0.01),
        "a_cmp_w2": nrm(ks[16], (N_A, 2, CMP_HIDDEN, HEAD_DIM), CMP_HIDDEN ** -0.5),
        "a_cmp_b2": nrm(ks[17], (N_A, 2, HEAD_DIM), 0.01),
        "b_w_in": nrm(ks[18], (N_B, D_MODEL, B_IN), D_MODEL ** -0.5),
        "kv_norm": 1.0 + nrm(ks[19], (D_MODEL,), 0.02),
        "w_kv_shared": nrm(ks[20], (D_MODEL, SHARED_W), D_MODEL ** -0.5),
        "b_fgate": 3.0 + nrm(ks[21], (N_MIX_HEADS,), 0.1),
        "final_norm": 1.0 + nrm(ks[22], (D_MODEL,), 0.02),
    }

def first_block(x, mem, attn_norm, ffn_norm, mem_norm, w_mem_kv, w_o, w_up, conv_w, conv_b, w_down,
              a_w_in, a_gate_b, a_cmp_pos, a_cmp_w1, a_cmp_b1, a_cmp_w2, a_cmp_b2,
              b_w_in, kv_norm, w_kv_shared, b_fgate, final_norm):
    B, S, _ = x.shape
    pos = jnp.arange(S)
    k_sh = v_sh = dcum = None
    for l in range(DEPTH):
        h = rms_norm(x, attn_norm[l])
        if l < N_A:
            o_mix, q_mem = nsa_mixer(h, a_w_in[l], a_gate_b[l], a_cmp_pos[l], a_cmp_w1[l], a_cmp_b1[l],
                                     a_cmp_w2[l], a_cmp_b2[l], pos)
        else:
            if l == N_A:
                hs = rms_norm(x, kv_norm) @ w_kv_shared
                k_sh = hs[..., :MIX_W].reshape(B, S, N_MIX_HEADS, HEAD_DIM)
                v_sh = hs[..., MIX_W:2 * MIX_W].reshape(B, S, N_MIX_HEADS, HEAD_DIM)
                log_f = jax.nn.log_sigmoid(hs[..., 2 * MIX_W:].astype(jnp.float32) + b_fgate.astype(jnp.float32))
                dcum = jnp.cumsum(log_f, axis=1).transpose(0, 2, 1)
            proj = h @ b_w_in[l - N_A]
            q = proj[..., :MIX_W].reshape(B, S, N_MIX_HEADS, HEAD_DIM)
            q_mem = proj[..., MIX_W:].reshape(B, S, N_MEM_HEADS, HEAD_DIM)
            o_mix = forgetting_attention(q, k_sh, v_sh, dcum)
        o_mem = memory_attention(q_mem, mem, mem_norm[l], w_mem_kv[l])
        x = x + jnp.concatenate([o_mix, o_mem], axis=-1) @ w_o[l]
        x = x + conv_ffn(rms_norm(x, ffn_norm[l]), w_up[l], conv_w[l], conv_b[l], w_down[l])
    return rms_norm(x, final_norm)


GRID_W = 64
CTX_LEN = 256
N_MIXERS = 3
NORM_EPS = 1e-6
N_MOD = 6
MLA_HEADS = 8
MLA_Q_LORA = 512
MLA_KV_LORA = 256
MLA_NOPE = 128
MLA_ROPE = 64
MLA_V = 128
CONV_DIM = D_MODEL
GQA_HEADS = 16
GQA_KV_HEADS = 8
GQA_HEAD_DIM = 128
MOE_GROUPS = 4
MOE_EXPERTS_PER_GROUP = 8
MOE_EXPERTS = MOE_GROUPS * MOE_EXPERTS_PER_GROUP
MOE_TOP_K = 2
MOE_FF = 512
MOE_BLOCK = 128


def _n_layers_of(kind):
    return len(range(kind, DEPTH, N_MIXERS))

def _rmsnorm(x, g):
    xf = x.astype(jnp.float32)
    y = xf * lax.rsqrt(jnp.mean(xf * xf, axis=-1, keepdims=True) + NORM_EPS)
    return (y * g.astype(jnp.float32)).astype(x.dtype)

def _modulate(x, g, shift, scale):
    return _rmsnorm(x, g) * (1 + scale) + shift

def _rope_1d(x, pos):
    half = x.shape[-1] // 2
    inv_freq = ROPE_THETA ** (-jnp.arange(half, dtype=jnp.float32) / half)
    ang = pos.astype(jnp.float32)[:, None] * inv_freq[None, :]
    cos, sin = jnp.cos(ang)[:, None, :], jnp.sin(ang)[:, None, :]
    xf = x.astype(jnp.float32)
    x1, x2 = xf[..., :half], xf[..., half:]
    return jnp.concatenate([x1 * cos - x2 * sin, x1 * sin + x2 * cos], axis=-1).astype(x.dtype)

def _axial_rope(x, rows, cols):
    half = x.shape[-1] // 2
    return jnp.concatenate([_rope_1d(x[..., :half], rows), _rope_1d(x[..., half:], cols)], axis=-1)

def _attend(q, k, v, scale):
    B, n, H, dk = q.shape
    Hk, dv = k.shape[2], v.shape[-1]
    G = H // Hk
    nb = n // Q_BLOCK
    qb = q.reshape(B, nb, Q_BLOCK, Hk, G, dk).transpose(1, 0, 2, 3, 4, 5)

    def block(qblk):
        s = jnp.einsum("bqhgd,bkhd->bhgqk", qblk, k).astype(jnp.float32) * scale
        p = jax.nn.softmax(s, axis=-1).astype(v.dtype)
        return jnp.einsum("bhgqk,bkhd->bqhgd", p, v)

    o = lax.map(block, qb)
    return o.transpose(1, 0, 2, 3, 4, 5).reshape(B, n, H * dv)

def _mla_project(a, w_dq, g_q, w_uq, w_dkv, g_kv, w_ukv, pos, want_q):
    B, n, _ = a.shape
    ckv = a @ w_dkv
    c_kv = _rmsnorm(ckv[..., :MLA_KV_LORA], g_kv)
    k_pe = ckv[..., MLA_KV_LORA:][:, :, None, :]
    kv = (c_kv @ w_ukv).reshape(B, n, MLA_HEADS, MLA_NOPE + MLA_V)
    k_nope, v = kv[..., :MLA_NOPE], kv[..., MLA_NOPE:]
    if pos is not None:
        k_pe = _axial_rope(k_pe, *pos)
    k = jnp.concatenate([k_nope, jnp.broadcast_to(k_pe, (B, n, MLA_HEADS, MLA_ROPE))], axis=-1)
    q = None
    if want_q:
        cq = _rmsnorm(a @ w_dq, g_q)
        q = (cq @ w_uq).reshape(B, n, MLA_HEADS, MLA_NOPE + MLA_ROPE)
        if pos is not None:
            q = jnp.concatenate([q[..., :MLA_NOPE], _axial_rope(q[..., MLA_NOPE:], *pos)], axis=-1)
    return q, k, v

def _mla(a_lat, a_ctx, pos, ctx_out, w_dq, g_q, w_uq, w_dkv, g_kv, w_ukv, w_o):
    scale = (MLA_NOPE + MLA_ROPE) ** -0.5
    q_l, k_l, v_l = _mla_project(a_lat, w_dq, g_q, w_uq, w_dkv, g_kv, w_ukv, pos, True)
    q_c, k_c, v_c = _mla_project(a_ctx, w_dq, g_q, w_uq, w_dkv, g_kv, w_ukv, None, ctx_out)
    k_all = jnp.concatenate([k_c, k_l], axis=1)
    v_all = jnp.concatenate([v_c, v_l], axis=1)
    y_lat = _attend(q_l, k_all, v_all, scale) @ w_o
    y_ctx = _attend(q_c, k_c, v_c, scale) @ w_o if ctx_out else None
    return y_lat, y_ctx

def _short_conv_seq(a, w_in, conv_w, w_out):
    bcu = a @ w_in
    b_gate, c_gate, u = jnp.split(bcu, 3, axis=-1)
    z = lax.conv_general_dilated(
        c_gate * u, conv_w[:, None, :], window_strides=(1,),
        padding=[((CONV_WIDTH - 1) // 2, (CONV_WIDTH - 1) // 2)],
        dimension_numbers=("NWC", "WIO", "NWC"), feature_group_count=CONV_DIM)
    return (b_gate * z) @ w_out

def _short_conv(a_lat, a_ctx, ctx_out, w_in, conv_w, w_out):
    y_lat = _short_conv_seq(a_lat, w_in, conv_w, w_out)
    y_ctx = _short_conv_seq(a_ctx, w_in, conv_w, w_out) if ctx_out else None
    return y_lat, y_ctx

def _gqa_project(a, w_qkv, q_g, k_g, pos, want_q):
    B, n, _ = a.shape
    dq = GQA_HEADS * GQA_HEAD_DIM
    dkv = GQA_KV_HEADS * GQA_HEAD_DIM
    kv = a @ w_qkv[:, dq:]
    k = _rmsnorm(kv[..., :dkv].reshape(B, n, GQA_KV_HEADS, GQA_HEAD_DIM), k_g)
    v = kv[..., dkv:].reshape(B, n, GQA_KV_HEADS, GQA_HEAD_DIM)
    if pos is not None:
        k = _axial_rope(k, *pos)
    q = None
    if want_q:
        q = _rmsnorm((a @ w_qkv[:, :dq]).reshape(B, n, GQA_HEADS, GQA_HEAD_DIM), q_g)
        if pos is not None:
            q = _axial_rope(q, *pos)
    return q, k, v

def _gqa(a_lat, a_ctx, pos, ctx_out, w_qkv, q_g, k_g, w_o):
    scale = GQA_HEAD_DIM ** -0.5
    q_l, k_l, v_l = _gqa_project(a_lat, w_qkv, q_g, k_g, pos, True)
    q_c, k_c, v_c = _gqa_project(a_ctx, w_qkv, q_g, k_g, None, ctx_out)
    k_all = jnp.concatenate([k_c, k_l], axis=1)
    v_all = jnp.concatenate([v_c, v_l], axis=1)
    y_lat = _attend(q_l, k_all, v_all, scale) @ w_o
    y_ctx = _attend(q_c, k_c, v_c, scale) @ w_o if ctx_out else None
    return y_lat, y_ctx

def _hier_moe(h, w_group, b_group, w_expert, b_expert, w_gate, w_up, w_down):
    T, D = h.shape
    hf = h.astype(jnp.float32)
    g_prob = jax.nn.softmax(hf @ w_group.astype(jnp.float32), axis=-1)
    g_sel = jnp.argmax(g_prob + b_group.astype(jnp.float32), axis=-1)
    g_w = jnp.take_along_axis(g_prob, g_sel[:, None], axis=-1)
    e_logits = (hf @ w_expert.astype(jnp.float32)).reshape(T, MOE_GROUPS, MOE_EXPERTS_PER_GROUP)
    e_prob = jax.nn.softmax(jnp.take_along_axis(e_logits, g_sel[:, None, None], axis=1)[:, 0], axis=-1)
    e_bias = b_expert.astype(jnp.float32).reshape(MOE_GROUPS, MOE_EXPERTS_PER_GROUP)[g_sel]
    _, top_idx = lax.top_k(e_prob + e_bias, MOE_TOP_K)
    top_w = jnp.take_along_axis(e_prob, top_idx, axis=-1)
    top_w = top_w / jnp.sum(top_w, axis=-1, keepdims=True) * g_w
    expert_id = g_sel[:, None] * MOE_EXPERTS_PER_GROUP + top_idx

    A = T * MOE_TOP_K
    eid = expert_id.reshape(A)
    tok = jnp.arange(A, dtype=jnp.int32) // MOE_TOP_K
    wts = top_w.reshape(A)
    order = jnp.argsort(eid)
    e_s, tok_s, w_s = eid[order], tok[order], wts[order]
    counts = jnp.bincount(eid, length=MOE_EXPERTS)
    starts = jnp.cumsum(counts) - counts
    padded = (counts + MOE_BLOCK - 1) // MOE_BLOCK * MOE_BLOCK
    pends = jnp.cumsum(padded)
    pstarts = pends - padded
    dest = pstarts[e_s] + (jnp.arange(A, dtype=jnp.int32) - starts[e_s])
    nb = -(-A // MOE_BLOCK) + MOE_EXPERTS
    xp = jnp.zeros((nb * MOE_BLOCK, D), h.dtype).at[dest].set(h[tok_s])
    blk_e = jnp.clip(jnp.searchsorted(pends, jnp.arange(nb, dtype=jnp.int32) * MOE_BLOCK, side="right"),
                     0, MOE_EXPERTS - 1)

    def expert_block(args):
        xb, e = args
        return (jax.nn.silu(xb @ w_gate[e]) * (xb @ w_up[e])) @ w_down[e]

    yp = lax.map(expert_block, (xp.reshape(nb, MOE_BLOCK, D), blk_e)).reshape(nb * MOE_BLOCK, D)
    return jax.ops.segment_sum(yp[dest] * w_s[:, None].astype(h.dtype), tok_s, num_segments=T)

def _normal(k, shape, scale):
    return jax.random.normal(k, shape, jnp.float32) * scale

def second_inputs(seed: int = 0) -> dict:
    key = jax.random.key(seed)
    ks = iter(jax.random.split(key, 40))
    D = D_MODEL
    nA, nB, nC = _n_layers_of(0), _n_layers_of(1), _n_layers_of(2)
    dq = GQA_HEADS * GQA_HEAD_DIM
    dkv = GQA_KV_HEADS * GQA_HEAD_DIM
    return {
        "x": _normal(next(ks), (BATCH, SEQ, D), 1.0),
        "c": _normal(next(ks), (BATCH, D), 1.0),
        "ctx": _normal(next(ks), (BATCH, CTX_LEN, D), 1.0),
        "c_ctx": _normal(next(ks), (D,), 1.0),
        "w_mod": _normal(next(ks), (DEPTH, D, N_MOD * D), 0.5 * D ** -0.5),
        "b_mod": _normal(next(ks), (DEPTH, N_MOD * D), 0.02),
        "norm_mix_g": 1.0 + _normal(next(ks), (DEPTH, D), 0.05),
        "norm_ffn_g": 1.0 + _normal(next(ks), (DEPTH, D), 0.05),
        "mla_w_dq": _normal(next(ks), (nA, D, MLA_Q_LORA), D ** -0.5),
        "mla_g_q": 1.0 + _normal(next(ks), (nA, MLA_Q_LORA), 0.05),
        "mla_w_uq": _normal(next(ks), (nA, MLA_Q_LORA, MLA_HEADS * (MLA_NOPE + MLA_ROPE)), MLA_Q_LORA ** -0.5),
        "mla_w_dkv": _normal(next(ks), (nA, D, MLA_KV_LORA + MLA_ROPE), D ** -0.5),
        "mla_g_kv": 1.0 + _normal(next(ks), (nA, MLA_KV_LORA), 0.05),
        "mla_w_ukv": _normal(next(ks), (nA, MLA_KV_LORA, MLA_HEADS * (MLA_NOPE + MLA_V)), MLA_KV_LORA ** -0.5),
        "mla_w_o": _normal(next(ks), (nA, MLA_HEADS * MLA_V, D), (MLA_HEADS * MLA_V) ** -0.5),
        "conv_w_in": _normal(next(ks), (nB, D, 3 * CONV_DIM), D ** -0.5),
        "conv_w": _normal(next(ks), (nB, CONV_WIDTH, CONV_DIM), CONV_WIDTH ** -0.5),
        "conv_w_out": _normal(next(ks), (nB, CONV_DIM, D), CONV_DIM ** -0.5),
        "gqa_w_qkv": _normal(next(ks), (nC, D, dq + 2 * dkv), D ** -0.5),
        "gqa_q_norm_g": 1.0 + _normal(next(ks), (nC, GQA_HEAD_DIM), 0.05),
        "gqa_k_norm_g": 1.0 + _normal(next(ks), (nC, GQA_HEAD_DIM), 0.05),
        "gqa_w_o": _normal(next(ks), (nC, dq, D), dq ** -0.5),
        "moe_w_group": _normal(next(ks), (DEPTH, D, MOE_GROUPS), D ** -0.5),
        "moe_b_group": _normal(next(ks), (DEPTH, MOE_GROUPS), 0.01),
        "moe_w_expert": _normal(next(ks), (DEPTH, D, MOE_EXPERTS), D ** -0.5),
        "moe_b_expert": _normal(next(ks), (DEPTH, MOE_EXPERTS), 0.01),
        "moe_w_gate": _normal(next(ks), (DEPTH, MOE_EXPERTS, D, MOE_FF), D ** -0.5),
        "moe_w_up": _normal(next(ks), (DEPTH, MOE_EXPERTS, D, MOE_FF), D ** -0.5),
        "moe_w_down": _normal(next(ks), (DEPTH, MOE_EXPERTS, MOE_FF, D), MOE_FF ** -0.5),
        "final_norm_g": 1.0 + _normal(next(ks), (D,), 0.05),
    }

def second_block(x, c, ctx, c_ctx, w_mod, b_mod, norm_mix_g, norm_ffn_g,
              mla_w_dq, mla_g_q, mla_w_uq, mla_w_dkv, mla_g_kv, mla_w_ukv, mla_w_o,
              conv_w_in, conv_w, conv_w_out,
              gqa_w_qkv, gqa_q_norm_g, gqa_k_norm_g, gqa_w_o,
              moe_w_group, moe_b_group, moe_w_expert, moe_b_expert, moe_w_gate, moe_w_up, moe_w_down,
              final_norm_g):
    B, S, D = x.shape
    L = ctx.shape[1]
    ROWS = S // GRID_W
    rows = jnp.repeat(jnp.arange(ROWS, dtype=jnp.int32), GRID_W)
    cols = jnp.tile(jnp.arange(GRID_W, dtype=jnp.int32), ROWS)
    pos = (rows, cols)
    cond_lat = jax.nn.silu(c)
    cond_ctx = jax.nn.silu(c_ctx)[None]
    h = ctx
    for i in range(DEPTH):
        kind, j = i % N_MIXERS, i // N_MIXERS
        ctx_out = i < DEPTH - 1
        mod_l = (cond_lat @ w_mod[i] + b_mod[i])[:, None, :]
        mod_c = (cond_ctx @ w_mod[i] + b_mod[i])[:, None, :]
        sh1, sc1, g1, sh2, sc2, g2 = jnp.split(mod_l, N_MOD, axis=-1)
        csh1, csc1, cg1, csh2, csc2, cg2 = jnp.split(mod_c, N_MOD, axis=-1)
        a_lat = _modulate(x, norm_mix_g[i], sh1, sc1)
        a_ctx = _modulate(h, norm_mix_g[i], csh1, csc1)
        if kind == 0:
            y_lat, y_ctx = _mla(a_lat, a_ctx, pos, ctx_out, mla_w_dq[j], mla_g_q[j], mla_w_uq[j],
                                mla_w_dkv[j], mla_g_kv[j], mla_w_ukv[j], mla_w_o[j])
        elif kind == 1:
            y_lat, y_ctx = _short_conv(a_lat, a_ctx, ctx_out, conv_w_in[j], conv_w[j], conv_w_out[j])
        else:
            y_lat, y_ctx = _gqa(a_lat, a_ctx, pos, ctx_out, gqa_w_qkv[j], gqa_q_norm_g[j],
                                gqa_k_norm_g[j], gqa_w_o[j])
        x = x + g1 * y_lat
        f_lat = _modulate(x, norm_ffn_g[i], sh2, sc2)
        moe_args = (moe_w_group[i], moe_b_group[i], moe_w_expert[i], moe_b_expert[i],
                    moe_w_gate[i], moe_w_up[i], moe_w_down[i])
        if ctx_out:
            h = h + cg1 * y_ctx
            f_ctx = _modulate(h, norm_ffn_g[i], csh2, csc2)
            tokens = jnp.concatenate([f_lat.reshape(B * S, D), f_ctx.reshape(B * L, D)], axis=0)
            y = _hier_moe(tokens, *moe_args)
            x = x + g2 * y[:B * S].reshape(B, S, D)
            h = h + cg2 * y[B * S:].reshape(B, L, D)
        else:
            y = _hier_moe(f_lat.reshape(B * S, D), *moe_args)
            x = x + g2 * y.reshape(B, S, D)
    return _rmsnorm(x, final_norm_g)


def setup_inputs(seed=0):
    out = dict(first_inputs(seed))
    for name, value in second_inputs(seed + 1).items():
        if name != "x":
            out[name + "_2"] = value
    return out


def reference(
    x, mem, attn_norm, ffn_norm, mem_norm, w_mem_kv, w_o, w_up, conv_w, conv_b, w_down, a_w_in,
    a_gate_b, a_cmp_pos, a_cmp_w1, a_cmp_b1, a_cmp_w2, a_cmp_b2, b_w_in, kv_norm, w_kv_shared,
    b_fgate, final_norm, c_2, ctx_2, c_ctx_2, w_mod_2, b_mod_2, norm_mix_g_2, norm_ffn_g_2,
    mla_w_dq_2, mla_g_q_2, mla_w_uq_2, mla_w_dkv_2, mla_g_kv_2, mla_w_ukv_2, mla_w_o_2,
    conv_w_in_2, conv_w_2, conv_w_out_2, gqa_w_qkv_2, gqa_q_norm_g_2, gqa_k_norm_g_2, gqa_w_o_2,
    moe_w_group_2, moe_b_group_2, moe_w_expert_2, moe_b_expert_2, moe_w_gate_2, moe_w_up_2,
    moe_w_down_2, final_norm_g_2,
):
    x = first_block(
        x, mem, attn_norm, ffn_norm, mem_norm, w_mem_kv, w_o, w_up, conv_w, conv_b, w_down,
        a_w_in, a_gate_b, a_cmp_pos, a_cmp_w1, a_cmp_b1, a_cmp_w2, a_cmp_b2, b_w_in, kv_norm,
        w_kv_shared, b_fgate, final_norm,
    )
    return second_block(
        x, c_2, ctx_2, c_ctx_2, w_mod_2, b_mod_2, norm_mix_g_2, norm_ffn_g_2, mla_w_dq_2,
        mla_g_q_2, mla_w_uq_2, mla_w_dkv_2, mla_g_kv_2, mla_w_ukv_2, mla_w_o_2, conv_w_in_2,
        conv_w_2, conv_w_out_2, gqa_w_qkv_2, gqa_q_norm_g_2, gqa_k_norm_g_2, gqa_w_o_2,
        moe_w_group_2, moe_b_group_2, moe_w_expert_2, moe_b_expert_2, moe_w_gate_2, moe_w_up_2,
        moe_w_down_2, final_norm_g_2,
    )


_drawn_inputs = setup_inputs


def setup_inputs(seed=0):
    import zlib

    import numpy as np

    out = dict(_drawn_inputs(seed))
    spreads = {}
    factors = {'attn_norm': 3.7,
     'mem_norm': 8.0,
     'conv_b': 3.093,
     'a_gate_b': 8.0,
     'a_cmp_b1': 8.0,
     'a_cmp_b2': 4.691,
     'kv_norm': 3.705,
     'b_fgate': 32.208,
     'mla_g_q_2': 8.0,
     'mla_g_kv_2': 4.776,
     'moe_b_group_2': 20.368,
     'moe_b_expert_2': 10.257,
     'norm_ffn_g_2': 3.324}
    for name, (base, spread) in spreads.items():
        noise = np.random.default_rng([zlib.crc32(name.encode()), seed]).standard_normal(out[name].shape)
        drawn = base * np.exp(spread * noise) if base else spread * noise
        out[name] = __import__('jax').numpy.asarray(drawn.astype(out[name].dtype))
    for name, factor in factors.items():
        out[name] = (out[name] * factor).astype(out[name].dtype)
    return out
```

```python
from contextlib import ExitStack

import numpy as np

import concourse.bass as bass
from concourse import mybir

D = 1024
S = 256
L_CTX = 256
P = 128
KT = D // P
TC = S // P
EPS = 1e-6
DEPTH = 2
HD = 64
NH = 12
NG = 2
HPG = NH // NG
NM = 4
MIX_W = NH * HD
MEM_W = NM * HD
GATE_W = 3 * NH
KV0 = MIX_W
GATE0 = KV0 + 6 * NG * HD
QMEM0 = GATE0 + GATE_W
A_IN = QMEM0 + MEM_W
L_CMP, CMP_STRIDE, CMP_HID = 32, 16, 256
N_CMP = (S - L_CMP) // CMP_STRIDE + 1
SHARED_W = 2 * MIX_W + NH
D_FF = 2816
FT = D_FF // P
TAPS = 3
SCALE_A = HD ** -0.5
NEG = -1e30
N_MOD = 6
QL, KVL = 512, 256
MH, NOPE, ROPE, VD = 8, 128, 64, 128
SCALE_M = (NOPE + ROPE) ** -0.5
GRID_W = 64
G, EPG = 4, 8
E = G * EPG
FF = 512
SLOTS = 64
FFK = FF // P
GR = E // 2

CH = 4096
RING = 6
BANKS = 8
BW = 512


def n_pairs(tokens):
    return GR - 1 + 2 * tokens // SLOTS


NPAIR = n_pairs(S)
MOD_CHUNKS = N_MOD * D // BW


def stream_plan():
    plan = [("a_in", KT * min(BW, A_IN - i * BW)) for i in range(-(-A_IN // BW))]
    plan += [("mem0", CH)]
    plan += [("cmp", CH)] * 4
    plan += [("mod0", CH)] * MOD_CHUNKS
    plan += [("wo0", CH)] * 2
    plan += [("ffn0", KT * 256 + D)] * FT
    plan += [("b_in", CH)] * 2 + [("shared", KT * min(BW, SHARED_W - i * BW)) for i in range(4)]
    plan += [("mem1", CH)]
    plan += [("mod1", CH)] * MOD_CHUNKS
    plan += [("wo1", CH)] * 2
    plan += [("ffn1", KT * 256 + D)] * FT
    plan += [("dq", CH), ("dkv", KT * (KVL + ROPE)), ("uqn", CH), ("uqp", CH // 2), ("ukv", CH)]
    plan += [("mla_o", CH)] * 2
    plan += [("conv_in", KT * 384)] * KT + [("conv_out", CH)] * 2
    return plan


PLAN = stream_plan()


def first_of(name):
    return next(i for i, (n, _) in enumerate(PLAN) if n == name)


def count_of(name):
    return sum(n == name for n, _ in PLAN)


MOE_AT = [first_of("conv_in"), len(PLAN)]


def last_dense(n, slot):
    return n - 1 - (n - 1 - slot) % RING


def landed_at(n, experts_before=None):
    layers = int(n >= MOE_AT[0]) if experts_before is None else experts_before
    return 16 * (n // RING + 1) + 16 * GR * layers


def shape_constants():
    f = np.float32
    c = {}
    c["ident"] = np.eye(P, dtype=f)
    c["ones"] = np.ones((P, P), f)
    s_, t_ = np.arange(P)[:, None], np.arange(P)[None, :]
    c["before"] = (s_ < t_).astype(f)
    c["upto"] = (s_ <= t_).astype(f)
    causal = np.where(t_ <= s_, 0.0, NEG).astype(f)
    c["causal"] = np.concatenate([np.zeros((P, P), f), causal], 1)
    half = HD // 2
    inv = (f(10000.0) ** (-np.arange(half, dtype=f) / f(half))).astype(f)
    ang = np.arange(S, dtype=f)[:, None] * inv[None, :]
    cs = np.stack([np.cos(ang), np.sin(ang)], 1).astype(f)
    c["rope"] = cs.reshape(TC, P, 2 * half).transpose(1, 0, 2).reshape(P, -1)
    end = (np.arange(N_CMP) * CMP_STRIDE + L_CMP - 1)
    rc = np.zeros((P, 2 * half), f)
    rc[:NG * N_CMP] = np.tile(cs[end].reshape(N_CMP, -1), (NG, 1))
    c["rope_cmp"] = rc
    seen = (end[None, :] <= np.arange(S)[:, None])
    c["cmp_bias"] = np.where(seen, 0.0, NEG).astype(f).reshape(TC, P, N_CMP).transpose(1, 0, 2).reshape(P, -1)
    c["cmp_seen"] = seen.astype(f).reshape(TC, P, N_CMP).transpose(1, 0, 2).reshape(P, -1)
    q = 16
    inv = (f(10000.0) ** (-np.arange(q, dtype=f) / f(q))).astype(f)
    pos = np.stack([np.arange(S) // GRID_W, np.arange(S) % GRID_W], 1).astype(f)
    ang = pos[:, :, None] * inv
    ax = np.stack([np.cos(ang), np.sin(ang)], 1).astype(f)
    c["axial"] = ax.reshape(TC, P, 64).transpose(1, 0, 2).reshape(P, -1)
    q = np.zeros((P, 2), f)
    q[0::P // 4, 0] = q[1::P // 4, 1] = 1.0
    c["quarters"] = q
    n = NG * N_CMP
    c["fold"] = (s_ % (P // 4) == np.arange(n)[None, :]).astype(f)
    c["iota"] = np.tile(np.arange(P, dtype=f), (P, 1))
    e = np.arange(E)
    r = np.zeros((P, 5, E), f)
    r[:E, 0] = (e[:, None] // 2 < e[None, :] // 2) & (e[:, None] % 2 == 0)
    r[:E, 1] = (e[:, None] % 2 == 0)
    r[:, 2] = e // 2
    r[:, 3] = (e % 2) * SLOTS
    r[:, 4] = (np.arange(P) // 2 + 1)[:, None]
    c["router"] = r
    c["tokid"] = (np.arange(4)[None, :] * P + np.arange(P)[:, None]).astype(f)
    sel = np.zeros((P, NH, P), f)
    for h in range(NH):
        sel[h, h, :] = 1.0
    c["sel"] = sel.reshape(P, -1)
    return c


CONST_W = {"ident": P, "ones": P, "before": P, "causal": 2 * P, "axial": 128, "iota": P, "tokid": 4}
SMALL_W = {"gcols": KT * 7, "modg": KT * 4, "g_q": QL // P, "g_kv": KVL // P, "ccol": KT * 2, "conv3": KT * TAPS,
           "b_fgate": NH, "quarters": 2}


def two_blocks(nc, dram, out_x):
    fp32, bf16, i32 = mybir.dt.float32, mybir.dt.bfloat16, mybir.dt.int32
    ALU = mybir.AluOpType
    ACT = mybir.ActivationFunctionType
    AX = mybir.AxisListType
    ctx = ExitStack()
    with ctx:
        def sb(name, shape, dt=fp32):
            return ctx.enter_context(nc.sbuf_tensor(name, shape, dt))

        ring = sb("ring", [P, RING, CH])
        x_res = sb("x_res", [P, TC, D])
        c_res = sb("c_res", [P, TC, D])
        hT = sb("hT", [P, KT, 4 * P])
        WORK = 18944
        work = sb("work", [P, WORK])
        const = {n: sb("c_" + n, [P, w]) for n, w in CONST_W.items()}
        small = {n: sb("s_" + n, [P, w]) for n, w in SMALL_W.items()}
        mod = sb("mod", [P, DEPTH, N_MOD * KT, 2])
        gs = sb("gs", [P, KT, 2])
        sums, var, rvar, rstd = (sb(n, [P, 4]) for n in ("sums", "var", "rvar", "rstd"))
        mx, nmx, psums, pinv = (sb(n, [P, 2, 2]) for n in ("mx", "nmx", "psums", "pinv"))
        dest_i = sb("dest_i", [P, 2, 4], i32)
        wts = sb("wts", [P, 2, 4])
        ps = ctx.enter_context(nc.psum_tensor("ps", [P, BANKS, BW], fp32))
        f_rows = nc.dram_tensor("f_rows", [S, D], fp32, kind="Internal").ap()
        y_rows = nc.dram_tensor("y_rows", [NPAIR * P, D], fp32, kind="Internal").ap()

        def area(lo, *shape, parts=P):
            n = int(np.prod(shape))
            assert lo + n <= WORK, (lo, shape)
            v = work[0:parts, lo:lo + n]
            names = "abcd"[:len(shape)]
            if len(shape) == 1:
                return v
            return v.rearrange(f"p ({' '.join(names)}) -> p {' '.join(names)}", **dict(zip(names, shape)))

        class Signal:
            def __init__(self, name):
                self.sem = ctx.enter_context(nc.semaphore(name))
                self.used = 0

            def span(self, n):
                s = Span(self.sem, self.used, n)
                self.used += n
                return s

        class Span:

            def __init__(self, sem, base, n):
                self.sem, self.base, self.n = sem, base, n
                self.end = base + n

            def at(self, k):
                return k + self.base

        slot_full = [ctx.enter_context(nc.semaphore(f"slot_full{i}")) for i in range(RING)]
        chunk_used = ctx.enter_context(nc.semaphore("chunk_used"))
        const_loaded = ctx.enter_context(nc.semaphore("const_loaded"))
        x_loaded = ctx.enter_context(nc.semaphore("x_loaded"))
        mem_loaded = ctx.enter_context(nc.semaphore("mem_loaded"))
        ctx_loaded = ctx.enter_context(nc.semaphore("ctx_loaded"))
        stored = ctx.enter_context(nc.semaphore("stored"))
        act_step = ctx.enter_context(nc.semaphore("act_step"))
        dve_step = ctx.enter_context(nc.semaphore("dve_step"))
        K = {n: Signal(n) for n in (
            "squares_done", "squares_summed", "rvar_done", "rstd_done", "rows_scaled", "banks_ready", "act_evac", "dve_evac",
            "scores_ready", "max_done", "exp_done", "probs_done", "probsT_ready", "probsT_done", "out_ready",
            "out_done", "cmp_ready", "cmp_sub", "cmp_exp", "cmp_probs", "cmpT_ready", "cmpT_done",
            "up_ready", "up_copied", "conv_step", "conv_a", "conv_b", "silu_done", "gated", "aux_loaded",
            "rows_gathered0", "rows_gathered1", "xT_ready", "xT_done", "gate_ready", "upm_ready",
            "gate_silu", "hidden_done", "hT_ready", "hT_done", "down_ready", "down_done", "y_stored0", "y_stored1",
            "route_pe", "route_dve", "route_act", "f_stored", "y_fetched0", "y_fetched1", "combined", "diag_done",
            "mod_zeroed", "mod_ready", "mod_copied", "mod_summed")}
        chain = {"dve": 0, "act": 0}

        def link(v, ins):
            chain["dve"] += 1
            ins.then_inc(dve_step, 1)
            v.wait_ge(dve_step, chain["dve"])

        def linka(a, ins):
            chain["act"] += 1
            ins.then_inc(act_step, 1)
            a.wait_ge(act_step, chain["act"])

        def Stage(**counts):
            return {n: K[n].span(k) for n, k in counts.items()}

        def after(eng, *names):
            for name in names:
                for s in st[name].values():
                    if s.n:
                        eng.wait_ge(s.sem, s.end)

        XH = 16896
        xh = area(XH, 2, D)
        part_sums = area(XH, 4, D // 32)
        probs = area(XH, 2, BW)
        probsT = area(XH + 2 * BW, 2, 4, P)
        prod = area(XH, 2, BW)
        projA = area(0, TC, A_IN)
        gates = area(3656, TC, NH, 3)
        pcmp = area(3728, TC, NH, N_CMP)
        cst = area(4088, TC, NH, 2)
        w2sb = area(4136, 2, 2, HD)
        posT = area(4392, 2, L_CMP, parts=64)
        b1c = area(4456, 2, 2)
        b2r = area(4460, 2, HD)
        gate_br = area(4588, GATE_W)
        ropeT = area(4624, TC, 2, 32)
        rope_cmp = area(4752, 2, 32)
        cmp_bias = area(4816, TC, N_CMP)
        cmp_seen = area(4846, TC, N_CMP)
        hid = area(4876, 2, 2, NG * N_CMP)
        kcN = area(4996, HD)
        kcT = area(5060, NG * N_CMP)
        vcN = area(5090, NG, HD)
        kvmem = area(5304, TC, 2 * MEM_W)
        headsT = area(6328, 64, P, parts=64)
        B_Q, B_QM, B_KM, B_K = 0, 24, 32, 40
        B_CK = 48
        HT_END = 6328 + 56 * P
        bmod = area(HT_END + NH * 2 * P, DEPTH, N_MOD * KT)
        fold = area(HT_END + NH * 2 * P + DEPTH * N_MOD * KT, NG * N_CMP)
        assert HT_END + NH * 2 * P + DEPTH * N_MOD * KT + NG * N_CMP <= XH
        windows = area(HT_END, 2, L_CMP, NG * N_CMP, parts=64)
        pcT = area(HT_END, NH, 2 * P)
        rtmp4 = area(XH, 4, 384)
        projB = area(0, TC, D)
        shared = area(2048, TC, SHARED_W)
        LB = 6328 + 64 * P
        logf = area(LB, TC, NH)
        sgf = area(LB + 24, TC, NH)
        dcT = area(LB + 48, 2 * P)
        ndcT = area(LB + 304, 2 * P)
        upto = area(LB + 560, P)
        assert LB + 688 <= XH
        selr = hT[:, 0:6, 2 * P:4 * P]
        mod_rows = hT[:, 6:8, 2 * P:4 * P]
        oT = hT[:, :, 0:2 * P]
        U = area(0, 2, 2, S + 2)
        conv_ab = area(1032, 2, 2, S)
        sg = area(2056, 2, S)
        gT = area(2568, 2, S)
        convw = area(3080, 4, 2 * FT)
        qnT = area(0, MH, 4 * P)
        qpT = area(4096, MH, 4, P, parts=64)
        knT = area(8192, MH, 4 * P)
        vN = area(12288, 4, MH * VD)
        kpT = area(16384, 4, P, parts=64)
        cqN = area(12288, 4, QL)
        ckvN = area(14336, 4, KVL + ROPE)
        qpN = area(12288, 4, MH * ROPE)
        atmp = area(8192, 4, 256)
        cqT, ckvT, oM = hT[:, 0:4, :], hT[:, 4:6, :], hT
        gb = area(0, 2, D)
        diag = area(14336, KT, P)
        zT = area(4096, KT, S)
        cbuf = area(8192, 2, 2, S)
        cu = area(9216, 2, S + 2)
        cz = area(9732, 2, S)
        fg_row = area(0, D)
        xe = area(0, 2, D)
        xeT = area(2048, 2, KT, P)
        sgm = area(4096, 2, FF)
        hm = area(5120, 2, FF)
        hmT = area(6144, 2, FFK, P)
        ym = area(7168, 2, D)
        y01 = area(9216, 2, 2, D)
        fN = area(9216, 4, D)
        slot_i = area(13312, NPAIR).bitcast(i32)
        need_i = area(13344, E, parts=1).bitcast(i32)
        tab_i = area(13376, NPAIR, parts=1).bitcast(i32)
        RB = 14336
        lg = area(RB, 4, G + E)
        t32 = {n: area(RB + 144 + 128 * i, 4, G, EPG) for i, n in enumerate(("prod", "E0", "E1", "M", "P2"))}
        g4 = {n: area(RB + 784 + 16 * i, 4, G) for i, n in enumerate(("a", "e", "p", "b", "eq", "oh"))}
        e8 = {n: area(RB + 880 + 32 * i, 4, EPG) for i, n in enumerate(
            ("el", "e", "p", "b", "sc", "eq", "o0", "o1", "t"))}
        t1 = {n: area(RB + 1168 + 4 * i, 4) for i, n in enumerate(
            ("m", "s", "r", "gi", "gw", "m2", "s2", "r2", "i0", "w0", "i1", "w1", "ws", "wr"))}
        dst_f = area(RB + 1224, 2, 4)
        q_f = area(RB + 1232, 2, 4)
        b_f = area(RB + 1240, 2, 4)
        q_i = work[:, RB + 1248:RB + 1256].bitcast(i32).rearrange("p (a b) -> p a b", a=2)
        b_i = work[:, RB + 1256:RB + 1264].bitcast(i32).rearrange("p (a b) -> p a b", a=2)
        nbT = area(RB + 1264, P)
        pst = area(RB + 1392, E)
        pend = area(RB + 1424, 1)
        past = area(RB + 1425, NPAIR)
        onA = area(RB + 1473, 2, P)
        onB = area(RB + 1729, 2, NPAIR)
        wr = area(RB + 1792, KT, G + E)
        bg_r = area(RB + 2080, G)
        be_r = area(RB + 2084, G, EPG)
        rt = area(RB + 2116, 5, E)
        nbm = area(RB + 2276, P)
        rest = area(RB + 2404, E + 1)
        pad_f = area(RB + 2437, E + 1)
        pad_i = area(RB + 2470, E + 1).bitcast(i32)
        rk = area(RB + 2503, 2, 4)
        rk_f = area(RB + 2511, 2, 4)
        rk_i = work[:, RB + 2519:RB + 2527].bitcast(i32).rearrange("p (a b) -> p a b", a=2)
        assert RB + 2527 <= XH

        def squares(c, width):
            b = 4 + 2 * (c % 2)
            return ps[:, b:b + 2, :].rearrange("p a b -> p (a b)")[:, 0:width]

        def sel_row(h):
            return selr[0:NH, h // 2, (h % 2) * P:(h % 2 + 1) * P]

        def head_pairs(n):
            return [(j, c, h) for j in range(n // 2) for c in range(TC) for h in (2 * j, 2 * j + 1)]

        def nsa_items():
            items = []
            for j, c, h in head_pairs(NH):
                nk, g, q = (c + 1) * P, h // HPG, headsT[:, B_Q + h * TC + c, :]
                scores, regions, pv = [], [], []
                for b in range(2):
                    k0 = B_K + (b * NG + g) * TC
                    v0 = KV0 + (3 + 2 * b) * NG * HD + g * HD
                    scores.append((b * 256, nk, [(q, headsT[:, k0:k0 + c + 1, :])]))
                    regions.append((b * 256, nk, True, gates[:, c, h, b + 1:b + 2]))
                    pv += [(2 * b + t, projA[:, t, v0:v0 + HD]) for t in range(c + 1)]
                items.append(dict(scores=scores, regions=regions, pv=pv, scale=1.0,
                                  extra=[(vcN[0:N_CMP, g, :], pcT[0:N_CMP, h, c * P:(c + 1) * P])],
                                  part=(h % 2) * HD, m=HD, last=h % 2 == 1, dst=oT[:, j, c * P:(c + 1) * P]))
            return items

        def forget_items():
            items = []
            for j, c, h in head_pairs(NH):
                nk = (c + 1) * P
                sel = sel_row(h)
                wide = sel if c == 0 else sel.unsqueeze(1).broadcast_to([NH, TC, P])
                ms = [(headsT[:, B_Q + h * TC + c, :], headsT[:, B_K + h * TC:B_K + h * TC + c + 1, :]),
                      (dcT[0:NH, c * P:(c + 1) * P], wide), (sel, ndcT[0:NH, 0:nk])]
                items.append(dict(scores=[(0, nk, ms)], regions=[(0, nk, True, None)], scale=1.0,
                                  pv=[(t, shared[:, t, MIX_W + h * HD:MIX_W + (h + 1) * HD]) for t in range(c + 1)],
                                  extra=[], part=(h % 2) * HD, m=HD, last=h % 2 == 1,
                                  dst=oT[:, j, c * P:(c + 1) * P]))
            return items

        def mem_items():
            items = []
            for j, c, h in head_pairs(NM):
                k0 = B_KM + h * TC
                items.append(dict(scores=[(0, S, [(headsT[:, B_QM + h * TC + c, :], headsT[:, k0:k0 + TC, :])])],
                                  regions=[(0, S, False, None)], scale=1.0,
                                  pv=[(t, kvmem[:, t, MEM_W + h * HD:MEM_W + (h + 1) * HD]) for t in range(TC)],
                                  extra=[], part=(h % 2) * HD, m=HD, last=h % 2 == 1,
                                  dst=oT[:, NH // 2 + j, c * P:(c + 1) * P]))
            return items

        def mla_items():
            items = []
            for c in range(TC):
                t0, nt = 0, 4
                for h in range(MH):
                    ms = [(qnT[:, h, c * P:(c + 1) * P], knT[:, h, t0 * P:(t0 + nt) * P]),
                          (qpT[:, h, c, :], kpT[:, t0:t0 + nt, :])]
                    items.append(dict(scores=[(0, nt * P, ms)], regions=[(0, nt * P, False, None)], scale=SCALE_M,
                                      pv=[(t, vN[:, t0 + t, h * VD:(h + 1) * VD]) for t in range(nt)],
                                      extra=[], part=0, m=P, last=True, dst=oM[:, h, c * P:(c + 1) * P]))
            return items

        ATT = {"nsa": nsa_items() + mem_items(), "fgt": forget_items() + mem_items(), "mla": mla_items()}

        MOD_OF = {"nsa": 0, "fgt": 1, "mla": None}

        def mod_chunk(name, i):
            return i // 2 if MOD_OF[name] is not None and i % 2 == 0 and i // 2 < MOD_CHUNKS else None

        st = {}

        def norm_stage(name, T, width=D, same_rows=False):
            n, new = T * max(1, width // BW), int(not same_rows)
            st[name] = Stage(squares_done=T * new, squares_summed=T * new, rvar_done=new, rstd_done=new, rows_scaled=T,
                             banks_ready=n, dve_evac=n)

        def evac_stage(name, n):
            st[name] = Stage(banks_ready=n, act_evac=(n + 1) // 2, dve_evac=n // 2)

        def attn_stage(name):
            n = len(ATT[name])
            st[name] = Stage(scores_ready=n, max_done=n, exp_done=n, probs_done=n, probsT_ready=n, probsT_done=n,
                             out_ready=n, out_done=sum(it["last"] for it in ATT[name]))
            if MOD_OF[name] is not None:
                st[name + "_mod"] = Stage(mod_zeroed=1, mod_ready=MOD_CHUNKS, mod_copied=MOD_CHUNKS,
                                          mod_summed=MOD_CHUNKS, dve_evac=1)

        def ffn_stage(name):
            st[name] = Stage(aux_loaded=16, up_ready=FT, up_copied=FT, conv_step=4 * FT, conv_a=FT, conv_b=FT,
                             silu_done=FT, gated=FT, banks_ready=1, dve_evac=1)

        def gate_stage(name, streams):
            st[name] = Stage(diag_done=streams, banks_ready=2 * streams, act_evac=2 * streams)

        def expert_stages(T, tag):
            nb = n_pairs(T * P)
            st["frows" + tag] = Stage(banks_ready=2 * T, act_evac=T, dve_evac=T, f_stored=16 * T)
            st["route" + tag] = Stage(aux_loaded=64, route_pe=5 + 2 * T, route_dve=7 + 2 * T, route_act=2)
            st["moe" + tag] = Stage(
                rows_gathered0=8 * (nb + 1), rows_gathered1=8 * (nb - 1),
                xT_ready=2 * nb, xT_done=2 * nb, gate_ready=nb, upm_ready=nb, gate_silu=nb,
                hidden_done=nb, hT_ready=nb, hT_done=nb, down_ready=2 * nb, down_done=2 * nb,
                y_stored0=8 * (nb + 1), y_stored1=8 * (nb - 1))
            gate_stage("g2_" + tag, T // TC)
            st["comb" + tag] = Stage(y_fetched0=32 * (T // 2), y_fetched1=32 * (T // 2), combined=T)

        st["mod"] = Stage(route_act=1)
        norm_stage("normA0", TC)
        evac_stage("projA", -(-A_IN // BW) * TC)
        norm_stage("normM0", TC)
        evac_stage("mem0", TC)
        st["ropeA"] = Stage(dve_evac=2, act_evac=1)
        evac_stage("headsA", 56 // 4)
        st["cmp1"] = Stage(dve_evac=3, banks_ready=4, act_evac=2)
        st["cmp2"] = Stage(banks_ready=4, dve_evac=4)
        st["cmpatt"] = Stage(cmp_ready=TC, cmp_sub=TC, cmp_exp=TC, cmp_probs=TC, cmpT_ready=3 * TC, cmpT_done=3 * TC)
        attn_stage("nsa")
        st["wo0"] = Stage(banks_ready=2 * TC, dve_evac=2 * TC)
        norm_stage("normF0", TC)
        ffn_stage("ffn0")
        norm_stage("normA1", TC)
        evac_stage("b_in", 2 * TC)
        norm_stage("normS", TC, same_rows=True)
        evac_stage("shared", 4 * TC)
        norm_stage("normM1", TC)
        evac_stage("mem1", TC)
        st["dcum"] = Stage(aux_loaded=16, act_evac=2, banks_ready=1, dve_evac=4)
        evac_stage("headsB", 64 // 4)
        attn_stage("fgt")
        st["wo1"] = Stage(banks_ready=2 * TC, dve_evac=2 * TC)
        norm_stage("normF1", TC)
        ffn_stage("ffn1")
        st["end1"] = Stage(aux_loaded=16, squares_done=TC, squares_summed=TC, rvar_done=1, rstd_done=1, rows_scaled=TC)
        norm_stage("normX0", 4)
        evac_stage("mlaN", 8)
        st["kpe"] = Stage(dve_evac=1)
        evac_stage("kpeT", 1)
        norm_stage("normQ", 4, QL)
        norm_stage("normKV", 4, KVL)
        evac_stage("qn", MH)
        evac_stage("qp", 4)
        st["qrope"] = Stage(dve_evac=1)
        evac_stage("qpT", MH)
        evac_stage("ukv", MH + 8)
        attn_stage("mla")
        gate_stage("g1_0", 1)
        st["mla_o"] = Stage(banks_ready=2 * TC, dve_evac=2 * TC)
        norm_stage("normX1", TC)
        expert_stages(TC, "0")
        norm_stage("normX2", TC)
        st["conv"] = Stage(banks_ready=2 * KT, act_evac=KT, dve_evac=KT)
        gate_stage("g1_1", 1)
        st["conv_o"] = Stage(banks_ready=2 * TC, dve_evac=2 * TC)
        norm_stage("normX3", TC)
        expert_stages(TC, "1")
        st["final"] = Stage(aux_loaded=16, squares_done=TC, squares_summed=TC, rvar_done=1, rstd_done=1, rows_scaled=TC)

        def col(t, c, c0):
            return t[:, c, c0:c0 + HD]
        mem_k = [col(kvmem, c, h * HD) for h in range(NM) for c in range(TC)]
        HEADS_A = [col(projA, c, h * HD) for h in range(NH) for c in range(TC)]
        HEADS_A += [col(projA, c, QMEM0 + h * HD) for h in range(NM) for c in range(TC)] + mem_k
        HEADS_A += [col(projA, c, KV0 + ((2 + 2 * b) * NG + g) * HD) for b in range(2) for g in range(NG)
                    for c in range(TC)]
        HEADS_A += [col(projA, c, KV0 + (kind * NG + g) * HD) for kind in range(2) for g in range(NG)
                    for c in range(TC)]
        HEADS_B = [col(projB, c, h * HD) for h in range(NH + NM) for c in range(TC)] + mem_k
        HEADS_B += [col(shared, c, h * HD) for h in range(NH) for c in range(TC)]

        def rows_out(t, T, widths):
            lo = [sum(widths[:i]) for i in range(len(widths))]

            def at(i):
                w, c = i // T, i % T
                return t[:, c, lo[w]:lo[w] + widths[w]], ps[:, i % BANKS, 0:widths[w]], 1.0
            return at

        def widths(name):
            return [PLAN[first_of(name) + i][1] // KT for i in range(count_of(name))]

        def heads_out(i):
            return (headsT[:, 4 * i:4 * i + 4, :], ps[0:HD, i % BANKS, :].rearrange("p (a b) -> p a b", a=4),
                    SCALE_A if i < (NH + NM) * TC // 4 else 1.0)

        def mlaN_out(i):
            c = i % 4
            if i < 4:
                return cqN[:, c, :], ps[:, i, :], 1.0
            return ckvN[:, c, :], ps[:, i, 0:KVL + ROPE], 1.0

        def ukv_out(i):
            if i < MH:
                return knT[:, i, :], ps[:, i % BANKS, :], 1.0
            c, h = (i - MH) // 2, (i - MH) % 2
            return vN[:, c, h * BW:(h + 1) * BW], ps[:, i % BANKS, :], 1.0

        OUT = {"projA": rows_out(projA, TC, widths("a_in")), "mem0": rows_out(kvmem, TC, [BW]),
               "headsA": heads_out, "b_in": rows_out(projB, TC, [BW] * 2),
               "shared": rows_out(shared, TC, widths("shared")), "mem1": rows_out(kvmem, TC, [BW]),
               "headsB": heads_out, "mlaN": mlaN_out,
               "kpeT": lambda i: (kpT[:, :, :], ps[0:HD, 0, :].rearrange("p (a b) -> p a b", a=4), 1.0),
               "qn": lambda i: (qnT[:, i, :], ps[:, i, :], 1.0),
               "qp": lambda i: (qpN[:, i, :], ps[:, i, :], 1.0),
               "qpT": lambda i: (qpT[:, i, :, :], ps[0:HD, i, :].rearrange("p (a b) -> p a b", a=4), 1.0),
               "ukv": ukv_out,
               "frows0": lambda i: (fN[:, i // 2, (i % 2) * BW:(i % 2 + 1) * BW], ps[:, i % BANKS, :], 1.0)}
        OUT["frows1"] = OUT["frows0"]

        def lat(c):
            return x_res[:, c, :]

        def mem_rows(c):
            return c_res[:, c, :]

        def both(c):
            return x_res[:, c, :] if c < TC else c_res[:, c - TC, :]

        block = ctx.enter_context(nc.Block())

        @block.sync
        def _(sp):
            sp.dma_start(x_res[:], dram["x"].rearrange("(c p) d -> p c d", p=P)).then_inc(x_loaded, 16)
            sp.wait_ge(const_loaded, CONST_LOADS * 16)
            sp.dma_start(c_res[:], dram["mem"].rearrange("(c p) d -> p c d", p=P)).then_inc(mem_loaded, 16)

            def load(n):
                if MOE_AT[0] <= n < MOE_AT[0] + RING:
                    s = st["moe0"]
                    through = s[("gate_ready", "upm_ready", "down_ready")[(n % RING) // 2]]
                    sp.wait_ge(through.sem, through.end)
                elif n >= RING:
                    sp.wait_ge(chunk_used, n - RING + 1)
                name, w = PLAN[n]
                parts = HD if name == "cmp" else P
                sp.dma_start(ring[0:parts, n % RING, 0:w], dram["dense"][n, 0:parts, 0:w]).then_inc(slot_full[n % RING], 16)

            def load_run(n0, count):
                w = PLAN[n0][1]
                whole = count // RING
                if whole and n0 < RING:
                    for u in range(RING):
                        load(n0 + u)
                    n0, count, whole = n0 + RING, count - RING, whole - 1
                if whole:
                    with sp.Fori(0, whole) as i:
                        for u in range(RING):
                            sp.wait_ge(chunk_used, i * RING + (n0 + u - RING + 1))
                            sp.dma_start(ring[:, (n0 + u) % RING, 0:w],
                                         dram["dense"][bass.ds(i * RING + (n0 + u), 1), :, 0:w]
                                         .rearrange("a p n -> p (a n)")).then_inc(slot_full[(n0 + u) % RING], 16)
                for n in range(n0 + whole * RING, n0 + count):
                    load(n)

            def loads(*names):
                for name in names:
                    n0, count = first_of(name), count_of(name)
                    if count > 2 * RING:
                        load_run(n0, count)
                    else:
                        for n in range(n0, n0 + count):
                            load(n)

            def load_experts(layer, tag):
                s = st["moe" + tag]
                n0 = MOE_AT[layer]
                weights = [dram["w_gate"], dram["w_up"], dram["w_down"]]
                through = [(s["gate_ready"], 1), (s["upm_ready"], 1), (s["down_ready"], 2)]

                def put(kind, g):
                    for q in range(2):
                        sp.dma_start(ring[:, 2 * kind + q, :], weights[kind][bass.ds(g * 2 + (layer * E + q), 1), :, :]
                                     .rearrange("a p n -> p (a n)")).then_inc(slot_full[2 * kind + q], 16)

                for kind in range(3):
                    n = last_dense(n0, 2 * kind + 1)
                    sp.wait_ge(chunk_used, max(n, last_dense(n0, 2 * kind)) + 1)
                    put(kind, 0)
                after(sp, "route" + tag)
                with sp.Fori(1, GR) as g:
                    pairs = sp.value_load(need_i[0:1, bass.ds(g * 2, 1)], min_val=1, max_val=NPAIR)
                    for kind, (t, each) in enumerate(through):
                        sp.wait_ge(t.sem, pairs * each + t.base)
                        put(kind, g)

            loads("a_in", "mem0", "cmp", "mod0", "wo0", "ffn0", "b_in", "shared", "mem1", "mod1", "wo1", "ffn1")
            after(sp, "normM1")
            sp.dma_start(c_res[:], dram["ctx"].rearrange("(c p) d -> p c d", p=P)).then_inc(ctx_loaded, 16)
            loads("dq", "dkv", "uqn", "uqp", "ukv", "mla_o")
            load_experts(0, "0")
            loads("conv_in", "conv_out")
            load_experts(1, "1")
            f = st["final"]
            for c in range(TC):
                sp.wait_ge(f["rows_scaled"].sem, f["rows_scaled"].at(c + 1))
                sp.dma_start(out_x[c * P:(c + 1) * P, :], x_res[:, c, :]).then_inc(stored, 16)
            sp.wait_ge(stored, 16 * TC)
        @block.tensor
        def _(pe):
            owed = [0]

            def mm(out, lhsT, rhs, start, stop, done=None):
                ins = nc.tensor.matmul(out, lhsT, rhs, start=start, stop=stop)
                if done is not None:
                    ins.then_inc(done, 1)
                elif owed[0]:
                    ins.then_inc(chunk_used, 1)
                    owed[0] = 0

            def tr(out, rows, done=None):
                k = rows.shape[0]
                ins = nc.tensor.transpose(out, rows, const["ident"][0:k, 0:k])
                if done is not None:
                    ins.then_inc(done, 1)
                elif owed[0]:
                    ins.then_inc(chunk_used, 1)
                    owed[0] = 0

            nxt = [0]

            def take():
                n = nxt[0]
                nxt[0] += 1
                pe.wait_ge(slot_full[n % RING], landed_at(n))
                return ring[:, n % RING, :]

            def used():
                assert not owed[0]
                owed[0] = 1

            def bank_free(s, i, n=BANKS):
                if i >= n:
                    j = i - n
                    e = s["act_evac"] if j % 2 == 0 else s["dve_evac"]
                    pe.wait_ge(e.sem, e.at(j // 2 + 1))

            def norm(name, T, width=D):
                s = st[name]
                per = max(1, width // BW)
                kk = min(4, width // P)
                for c in range(T):
                    pe.wait_ge(s["rows_scaled"].sem, s["rows_scaled"].at(c + 1))
                    for h in range(per):
                        i = c * per + h
                        if i >= 4:
                            pe.wait_ge(s["dve_evac"].sem, s["dve_evac"].at(i - 3))
                        for k in range(kk):
                            tr(ps[:, i % 4, k * P:(k + 1) * P], xh[:, c % 2, (h * 4 + k) * P:(h * 4 + k + 1) * P],
                               s["banks_ready"].sem if k == kk - 1 else None)

            def rows_gemm(name, lhs, T, chunks, kt=KT, first=0):
                s = st[name]
                i = first
                for cols in chunks:
                    w = take()[:, 0:kt * cols].rearrange("p (k n) -> p k n", k=kt)
                    for c in range(T):
                        bank_free(s, i)
                        for k in range(kt):
                            mm(ps[:, i % BANKS, 0:cols], lhs(k, c), w[:, k, :], k == 0, k == kt - 1,
                               s["banks_ready"].sem if k == kt - 1 else None)
                        i += 1
                    used()

            def out_gemm(name, lhs, T):
                s = st[name]
                i = 0
                for half in range(2):
                    w = take()[:, :].rearrange("p (k n) -> p k n", k=KT)
                    for c in range(T):
                        if i >= BANKS:
                            pe.wait_ge(s["dve_evac"].sem, s["dve_evac"].at(i - BANKS + 1))
                        for k in range(KT):
                            mm(ps[:, i % BANKS, :], lhs(k, c), w[:, k, :], k == 0, k == KT - 1,
                               s["banks_ready"].sem if k == KT - 1 else None)
                        i += 1
                    used()

            def heads(name, blocks):
                s = st[name]
                for i in range(len(blocks) // 4):
                    bank_free(s, i)
                    for j in range(4):
                        tr(ps[0:HD, i % BANKS, j * P:(j + 1) * P], blocks[4 * i + j],
                           s["banks_ready"].sem if j == 3 else None)

            def attention(name):
                s, items = st[name], ATT[name]
                n = len(items)
                outs = [sum(it["last"] for it in items[:j]) for j in range(n)]
                if MOD_OF[name] is not None:
                    ms = st[name + "_mod"]
                    after(pe, "mod")
                    pe.wait_ge(ms["mod_zeroed"].sem, ms["mod_zeroed"].end)
                ccols = small["ccol"][:].rearrange("p (k s) -> p k s", s=2)
                for i in range(n + 2):
                    if i < n:
                        if i >= 2:
                            pe.wait_ge(s["exp_done"].sem, s["exp_done"].at(i - 1))
                        it = items[i]
                        groups = [(c0, nk, g) for c0, nk, g in it["scores"]]
                        for gi, (c0, nk, g) in enumerate(groups):
                            for mi, (l, r) in enumerate(g):
                                last = gi == len(groups) - 1 and mi == len(g) - 1
                                mm(ps[:, i % 2, c0:c0 + nk], l, r, mi == 0, mi == len(g) - 1,
                                   s["scores_ready"].sem if last else None)
                    m = mod_chunk(name, i)
                    if m is not None:
                        w = take().rearrange("p (k n) -> p k n", k=KT)
                        if m >= 1:
                            pe.wait_ge(ms["mod_copied"].sem, ms["mod_copied"].at(m))
                        for k in range(KT):
                            q = (k % 4) * (P // 4)
                            mm(ps[q:q + 2, 6, :], ccols[:, k, :], w[:, k, :], k < 4, k >= 4,
                               ms["mod_ready"].sem if k == KT - 1 else None)
                        used()
                    m = mod_chunk(name, i - 1)
                    if m is not None:
                        pe.wait_ge(ms["mod_copied"].sem, ms["mod_copied"].at(m + 1))
                        for t in range(BW // P):
                            o = (m * 4 + t) * 2
                            mm(ps[:, 7, o:o + 2], mod_rows[:, t // 2, (t % 2) * P:(t % 2 + 1) * P],
                               small["quarters"][:], True, True, ms["mod_summed"].sem if t == 3 else None)
                    j = i - 1
                    if 0 <= j < n:
                        pe.wait_ge(s["probs_done"].sem, s["probs_done"].at(j + 1))
                        if j >= 2:
                            pe.wait_ge(s["probsT_done"].sem, s["probsT_done"].at(j - 1))
                        tiles = [t for t, _ in items[j]["pv"]]
                        for t in tiles:
                            tr(ps[:, 2 + j % 2, t * P:(t + 1) * P], probs[:, j % 2, t * P:(t + 1) * P],
                               s["probsT_ready"].sem if t == tiles[-1] else None)
                    j = i - 2
                    if 0 <= j < n:
                        it = items[j]
                        pe.wait_ge(s["probsT_done"].sem, s["probsT_done"].at(j + 1))
                        o = outs[j]
                        if o >= 2:
                            pe.wait_ge(s["out_done"].sem, s["out_done"].at(o - 1))
                        prods = [(v, probsT[:, j % 2, t, :]) for t, v in it["pv"]] + it["extra"]
                        for q, (v, p) in enumerate(prods):
                            mm(ps[it["part"]:it["part"] + it["m"], 4 + o % 2, 0:P], v, p, q == 0,
                               q == len(prods) - 1, s["out_ready"].sem if q == len(prods) - 1 else None)

            def ffn(name):
                s = st[name]
                n0 = nxt[0]
                nxt[0] += FT

                def up(t, slot, w8, first):
                    pe.wait_ge(slot_full[slot % RING], w8)
                    if not first:
                        pe.wait_ge(s["up_copied"].sem, s["up_copied"].at(t - 1))
                    w = ring[:, slot % RING, 0:KT * 256].rearrange("p (k n) -> p k n", k=KT)
                    return w

                def products(w, par, rel):
                    for f in range(2):
                        for k in range(KT):
                            ins = nc.tensor.matmul(ps[:, par, f * S:(f + 1) * S], w[:, k, f * P:(f + 1) * P],
                                                   hT[:, k, 0:S], start=k == 0, stop=k == KT - 1)
                            if rel and f == 0 and k == 0:
                                ins.then_inc(chunk_used, 1)
                            if f == 1 and k == KT - 1:
                                ins.then_inc(s["up_ready"].sem, 1)

                def down(t, slot, par, start, stop):
                    pe.wait_ge(s["gated"].sem, s["gated"].at(t + 1))
                    w = ring[:, slot % RING, KT * 256:KT * 256 + D]
                    for c in range(TC):
                        for h in range(2):
                            ins = nc.tensor.matmul(ps[:, 4 + 2 * c + h, :], gT[:, par, c * P:(c + 1) * P],
                                                   w[:, h * BW:(h + 1) * BW], start=start, stop=stop)
                    ins.then_inc(s["banks_ready"].sem if stop else chunk_used, 1)

                rel = owed[0]
                owed[0] = 0
                products(up(0, n0, landed_at(n0), True), 0, rel)
                products(up(1, n0 + 1, landed_at(n0 + 1), True), 1, 0)
                down(0, n0, 0, True, False)
                whole = (FT - 2) // RING
                with pe.Fori(0, whole) as i:
                    for u in range(RING):
                        t = 2 + u
                        w = up(i * RING + t, n0 + t, i * 16 + landed_at(n0 + t), False)
                        products(w, u % 2, 0)
                        down(i * RING + (t - 1), n0 + t - 1, (u + 1) % 2, False, False)
                for t in range(2 + whole * RING, FT):
                    products(up(t, n0 + t, landed_at(n0 + t), False), t % 2, 0)
                    down(t - 1, n0 + t - 1, (t - 1) % 2, False, False)
                down(FT - 1, n0 + FT - 1, (FT - 1) % 2, False, True)
                owed[0] = 1

            def gate_rows(name, streams):
                s = st[name]
                for r in range(streams):
                    pe.wait_ge(s["diag_done"].sem, s["diag_done"].at(r + 1))
                    for h in range(2):
                        mm(ps[:, 2 * r + h, :], const["ones"][:], diag[:, 4 * h:4 * h + 4, :], True, True,
                           s["banks_ready"].sem)

            def feature_rows(name, T):
                s = st[name]
                for i in range(2 * T):
                    bank_free(s, i)
                    c, h = i // 2, i % 2
                    for k in range(4):
                        tr(ps[:, i % BANKS, k * P:(k + 1) * P], hT[:, 4 * h + k, c * P:(c + 1) * P],
                           s["banks_ready"].sem if k == 3 else None)

            def route(name, T):
                s = st[name]
                E0, E1, M = (t32[n].rearrange("p t g e -> p t (g e)") for n in ("E0", "E1", "M"))
                pe.wait_ge(s["aux_loaded"].sem, s["aux_loaded"].end)
                for c in range(T):
                    for k in range(KT):
                        mm(ps[:, 0, c * (G + E):(c + 1) * (G + E)], hT[:, k, c * P:(c + 1) * P], wr[:, k, :],
                           k == 0, k == KT - 1, s["route_pe"].sem if c == T - 1 and k == KT - 1 else None)
                pe.wait_ge(s["route_dve"].sem, s["route_dve"].at(3))
                for c in range(T):
                    for q in range(c + 1):
                        mm(ps[:, 1, c * E:(c + 1) * E], const["before" if q == c else "ones"][:], M[:, q, :],
                           q == 0, q == c)
                for c in range(T):
                    mm(ps[0:E, 2, 0:P], M[:, c, :], const["ones"][:], c == 0, c == T - 1,
                       s["route_pe"].sem if c == T - 1 else None)
                pe.wait_ge(s["route_dve"].sem, s["route_dve"].at(4))
                mm(ps[0:E, 7, 0:P], const["ident"][0:E, 1:E + 1], nbT[0:E, :], True, True, s["route_pe"].sem)
                pe.wait_ge(s["route_dve"].sem, s["route_dve"].at(5))
                mm(ps[:, 3, 0:E], nbm[0:E, :], rt[0:E, 0, :], True, True)
                mm(ps[:, 3, E:2 * E], nbm[0:E, :], rt[0:E, 1, :], True, True)
                mm(ps[0:E, 4, 0:1], rt[0:E, 0, :], nbm[0:E, 0:1], True, False)
                mm(ps[0:E, 4, 0:1], const["ident"][0:E, 0:E], nbm[0:E, 0:1], False, True)
                mm(ps[0:E, 4, 1:2], rt[0:E, 1, :], nbm[0:E, 0:1], True, True, s["route_pe"].sem)
                pe.wait_ge(s["route_dve"].sem, s["route_dve"].at(6))
                mm(ps[0:1, 5, 0:NPAIR], rt[0:E, 1, 0:1], past[0:E, :], True, True, s["route_pe"].sem)
                for r in range(2 * T):
                    pe.wait_ge(s["route_dve"].sem, s["route_dve"].at(6 + r + 1))
                    mm(ps[:, 6, 0:NPAIR], onA[:, r % 2, :], onB[:, r % 2, :], r == 0, r == 2 * T - 1,
                       s["route_pe"].sem)

            def experts(name, T):
                s = st[name]
                nb = n_pairs(T * P)
                layer = int(name[-1])
                n0 = nxt[0]
                fetched = [s["rows_gathered0"], s["rows_gathered1"]]
                assert not owed[0] and nb % 2 == 1

                def rows_T(b, i, par, first=False):
                    pe.wait_ge(fetched[par].sem, i * 16 + fetched[par].at(16))
                    for h in range(2):
                        if h == 0 and not first:
                            pe.wait_ge(s["xT_done"].sem, s["xT_done"].at(b * 2))
                        for k in range(4):
                            rows = xe[:, par, :].rearrange("t (p k) -> t k p", k=KT)[:, 4 * h + k, :]
                            ins = nc.tensor.transpose(ps[:, h, k * P:(k + 1) * P], rows, const["ident"][:])
                        ins.then_inc(s["xT_ready"].sem, 1)

                def landed(kind, loads):
                    for q in range(2):
                        before = landed_at(last_dense(n0, 2 * kind + q), layer)
                        pe.wait_ge(slot_full[2 * kind + q], loads + before)

                def products(bank, xT, kind, row, kk, c0, done):
                    for k in range(kk):
                        for q in range(2):
                            ins = nc.tensor.matmul(ps[q * SLOTS:(q + 1) * SLOTS, bank, :],
                                                   xT[:, k, q * SLOTS:(q + 1) * SLOTS],
                                                   ring[:, 2 * kind + q, k * row + c0:k * row + c0 + BW],
                                                   start=k == 0, stop=k == kk - 1)
                    ins.then_inc(done.sem, 1)

                def pair(b, i, par, first=False, more=True):
                    loads = pe.value_load(tab_i[0:1, bass.ds(b, 1)], min_val=16, max_val=16 * GR)
                    landed(0, loads)
                    pe.wait_ge(s["xT_done"].sem, s["xT_done"].at(b * 2 + 2))
                    if not first:
                        pe.wait_ge(s["gate_silu"].sem, s["gate_silu"].at(b))
                    products(2, xeT[:, par], 0, FF, KT, 0, s["gate_ready"])
                    landed(1, loads)
                    if not first:
                        pe.wait_ge(s["hidden_done"].sem, s["hidden_done"].at(b))
                    products(3, xeT[:, par], 1, FF, KT, 0, s["upm_ready"])
                    if more:
                        rows_T(b + 1, i + par, 1 - par)
                    pe.wait_ge(s["hidden_done"].sem, s["hidden_done"].at(b + 1))
                    for k in range(FFK):
                        rows = hm[:, par, :].rearrange("t (p k) -> t k p", k=FFK)[:, k, :]
                        ins = nc.tensor.transpose(ps[:, 4, k * P:(k + 1) * P], rows, const["ident"][:])
                    ins.then_inc(s["hT_ready"].sem, 1)
                    landed(2, loads)
                    pe.wait_ge(s["hT_done"].sem, s["hT_done"].at(b + 1))
                    for h in range(2):
                        if not first:
                            pe.wait_ge(s["down_done"].sem, s["down_done"].at(b * 2 - 1 + h))
                        products(5 + h, hmT[:, par], 2, D, FFK, h * BW, s["down_ready"])

                rows_T(0, 0, 0, first=True)
                pair(0, 0, 0, first=True)
                pair(1, 0, 1)
                with pe.Fori(1, nb // 2) as i:
                    for u in range(2):
                        pair(i * 2 + u, i, u)
                pair(nb - 1, nb // 2, 0, more=False)

            lhs = lambda k, c: hT[:, k, c * P:(c + 1) * P]
            lhs_o = lambda k, c: oT[:, k, c * P:(c + 1) * P]
            pe.wait_ge(const_loaded, CONST_LOADS * 16)
            norm("normA0", TC)
            after(pe, "normA0")
            rows_gemm("projA", lhs, TC, [PLAN[first_of("a_in") + i][1] // KT for i in range(count_of("a_in"))])
            after(pe, "projA")
            norm("normM0", TC)
            after(pe, "normM0")
            rows_gemm("mem0", lhs, TC, [BW])
            after(pe, "mem0", "ropeA")
            heads("headsA", HEADS_A)
            after(pe, "headsA")
            s = st["cmp1"]
            pe.wait_ge(s["dve_evac"].sem, s["dve_evac"].at(1))
            for kind in range(2):
                for half in range(2):
                    w = take()[0:HD, :].rearrange("p (j n) -> p j n", n=CMP_HID)
                    for j in range(16):
                        q = (j % 4) * (P // 4)
                        mm(ps[q:q + NG * N_CMP, 4 + kind, 0:CMP_HID], windows[:, kind, 16 * half + j, :], w[:, j, :],
                           half == 0 and j < 4, half == 1 and j >= 12,
                           s["banks_ready"].sem if half == 1 and j == 15 else None)
                    used()
            for kind in range(2):
                pe.wait_ge(s["dve_evac"].sem, s["dve_evac"].at(kind + 2))
                for t in range(2):
                    mm(ps[:, 2 * kind + t, 0:NG * N_CMP], mod_rows[:, kind, t * P:(t + 1) * P], fold, True, True,
                       s["banks_ready"].sem if t == 1 else None)
            s = st["cmp2"]
            after(pe, "cmp1")
            for t in range(2):
                mm(ps[0:NG * N_CMP, 4, 0:HD], hid[:, 0, t, :], w2sb[:, 0, t, :], t == 0, t == 1,
                   s["banks_ready"].sem if t else None)
            for g in range(NG):
                for t in range(2):
                    mm(ps[0:N_CMP, 5 + g, 0:HD], hid[:, 1, t, g * N_CMP:(g + 1) * N_CMP], w2sb[:, 1, t, :], t == 0,
                       t == 1, s["banks_ready"].sem if t else None)
            pe.wait_ge(s["dve_evac"].sem, s["dve_evac"].at(3))
            tr(ps[0:HD, 7, 0:NG * N_CMP], kcN[0:NG * N_CMP, :], s["banks_ready"].sem)
            s = st["cmpatt"]
            after(pe, "cmp2")
            for c in range(TC):
                for h in range(NH):
                    g = h // HPG
                    mm(ps[:, c, h * N_CMP:(h + 1) * N_CMP], headsT[:, B_Q + h * TC + c, :],
                       kcT[0:HD, g * N_CMP:(g + 1) * N_CMP], True, True, s["cmp_ready"].sem if h == NH - 1 else None)
            for c in range(TC):
                pe.wait_ge(s["cmp_probs"].sem, s["cmp_probs"].at(c + 1))
                for q in range(3):
                    for h in range(4 * q, 4 * q + 4):
                        tr(ps[0:N_CMP, 2 + 3 * c + q, (h % 4) * P:(h % 4 + 1) * P], pcmp[:, c, h, :],
                           s["cmpT_ready"].sem if h % 4 == 3 else None)
            after(pe, "cmpatt")
            attention("nsa")
            after(pe, "nsa", "nsa_mod")
            out_gemm("wo0", lhs_o, TC)
            after(pe, "wo0")
            norm("normF0", TC)
            after(pe, "normF0")
            ffn("ffn0")

            after(pe, "ffn0")
            norm("normA1", TC)
            after(pe, "normA1")
            rows_gemm("b_in", lhs, TC, [BW] * 2)
            after(pe, "b_in")
            norm("normS", TC)
            after(pe, "normS")
            rows_gemm("shared", lhs, TC, [PLAN[first_of("shared") + i][1] // KT for i in range(4)])
            after(pe, "shared")
            norm("normM1", TC)
            after(pe, "normM1")
            rows_gemm("mem1", lhs, TC, [BW])
            after(pe, "mem1")
            s = st["dcum"]
            pe.wait_ge(s["aux_loaded"].sem, s["aux_loaded"].end)
            pe.wait_ge(s["dve_evac"].sem, s["dve_evac"].at(2))
            mm(ps[0:NH, 0, 0:P], logf[:, 0, :], upto, True, True)
            mm(ps[0:NH, 0, P:2 * P], logf[:, 0, :], const["ones"][:], True, False)
            mm(ps[0:NH, 0, P:2 * P], logf[:, 1, :], upto, False, True, s["banks_ready"].sem)
            after(pe, "dcum")
            heads("headsB", HEADS_B)
            after(pe, "headsB")
            attention("fgt")
            after(pe, "fgt", "fgt_mod")
            out_gemm("wo1", lhs_o, TC)
            after(pe, "wo1")
            norm("normF1", TC)
            after(pe, "normF1")
            ffn("ffn1")

            after(pe, "ffn1", "end1")
            norm("normX0", 4)
            after(pe, "normX0")
            rows_gemm("mlaN", lhs, 4, [BW])
            rows_gemm("mlaN", lhs, 4, [KVL + ROPE], first=4)
            after(pe, "mlaN", "kpe")
            heads("kpeT", [ckvN[:, c, KVL:KVL + ROPE] for c in range(4)])
            after(pe, "kpeT")
            norm("normQ", 4, QL)
            after(pe, "normQ")
            norm("normKV", 4, KVL)
            after(pe, "normKV")
            s = st["qn"]
            w = take().rearrange("p (k n) -> p k n", k=QL // P)
            for h in range(MH):
                bank_free(s, h)
                for k in range(QL // P):
                    mm(ps[:, h, :], w[:, k, h * P:(h + 1) * P], cqT[:, k, :], k == 0, k == QL // P - 1,
                       s["banks_ready"].sem if k == QL // P - 1 else None)
            used()
            after(pe, "qn")
            rows_gemm("qp", lambda k, c: cqT[:, k, c * P:(c + 1) * P], 4, [BW], kt=QL // P)
            after(pe, "qp", "qrope")
            heads("qpT", [qpN[:, c, h * ROPE:(h + 1) * ROPE] for h in range(MH) for c in range(4)])
            after(pe, "qpT")
            s = st["ukv"]
            w = take().rearrange("p (k n) -> p k n", k=KVL // P)
            for i in range(MH + 8):
                bank_free(s, i)
                for k in range(2):
                    if i < MH:
                        l, r = w[:, k, i * P:(i + 1) * P], ckvT[:, k, :]
                    else:
                        c, h = (i - MH) // 2, (i - MH) % 2
                        l, r = ckvT[:, k, c * P:(c + 1) * P], w[:, k, D + h * BW:D + (h + 1) * BW]
                    mm(ps[:, i % BANKS, :], l, r, k == 0, k == 1, s["banks_ready"].sem if k else None)
            used()
            after(pe, "ukv")
            attention("mla")
            after(pe, "mla")
            gate_rows("g1_0", 1)
            after(pe, "g1_0")
            out_gemm("mla_o", lambda k, c: oM[:, k, c * P:(c + 1) * P], TC)
            after(pe, "mla_o")

            def moe(T, norm_name, tag):
                norm(norm_name, T)
                after(pe, norm_name)
                feature_rows("frows" + tag, T)
                after(pe, "frows" + tag)
                route("route" + tag, T)
                after(pe, "route" + tag)
                experts("moe" + tag, T)
                after(pe, "moe" + tag)
                gate_rows("g2_" + tag, T // TC)
                after(pe, "g2_" + tag, "comb" + tag)

            moe(TC, "normX1", "0")
            norm("normX2", TC)
            after(pe, "normX2")
            s = st["conv"]
            for t in range(KT):
                w = take()[:, 0:KT * 384].rearrange("p (k n) -> p k n", k=KT)
                for f in range(3):
                    i = 2 * t + (f == 2)
                    if f != 1:
                        bank_free(s, i)
                    o = f * S if f < 2 else 0
                    for k in range(KT):
                        mm(ps[:, i % BANKS, o:o + S], w[:, k, f * P:(f + 1) * P], hT[:, k, 0:S], k == 0,
                           k == KT - 1, s["banks_ready"].sem if f >= 1 and k == KT - 1 else None)
                used()
            after(pe, "conv")
            gate_rows("g1_1", 1)
            after(pe, "g1_1")
            out_gemm("conv_o", lambda k, c: zT[:, k, c * P:(c + 1) * P], TC)
            after(pe, "conv_o")
            moe(TC, "normX3", "1")

        @block.scalar
        def _(act):
            for name, dst in CONST_DST(const, small, dict(
                    bmod=bmod, w2=w2sb, posT=posT, b1=b1c, b2=b2r, gate_b=gate_br, rope=ropeT, rope_cmp=rope_cmp,
                    cmp_bias=cmp_bias, cmp_seen=cmp_seen, fold=fold), selr):
                act.dma_start(dst, dram[name]).then_inc(const_loaded, 16)

            def evac(name, n):
                s = st[name]
                for i in range(0, n, 2):
                    dst, src, factor = OUT[name](i)
                    act.wait_ge(s["banks_ready"].sem, s["banks_ready"].at(i + 1))
                    nc.scalar.activation(dst, src, ACT.Copy, scale=factor).then_inc(s["act_evac"].sem, 1)

            def norm(name, x, T, width=D):
                s = st[name]
                if not s["rstd_done"].n:
                    return
                for c in range(T):
                    if c >= 2:
                        act.wait_ge(s["squares_summed"].sem, s["squares_summed"].at(c - 1))
                    nc.scalar.activation(squares(c, width), x(c), ACT.Square).then_inc(s["squares_done"].sem, 1)
                act.wait_ge(s["rvar_done"].sem, s["rvar_done"].end)
                nc.scalar.activation(rstd[:, 0:T], rvar[:, 0:T], ACT.Sqrt).then_inc(s["rstd_done"].sem, 1)

            def closing_norm(name):
                s = st[name]
                for c in range(TC):
                    nc.scalar.activation(squares(c, D), x_res[:, c, :], ACT.Square).then_inc(s["squares_done"].sem, 1)
                act.wait_ge(s["rvar_done"].sem, s["rvar_done"].end)
                nc.scalar.activation(rstd[:, 0:TC], rvar[:, 0:TC], ACT.Sqrt).then_inc(s["rstd_done"].sem, 1)

            def attention(name):
                s, items = st[name], ATT[name]
                n = len(items)
                outs = [sum(it["last"] for it in items[:j]) for j in range(n)]
                for i in range(n + 2):
                    if i < n:
                        it = items[i]
                        act.wait_ge(s["max_done"].sem, s["max_done"].at(i + 1))
                        for r, (c0, nk, masked, _) in enumerate(it["regions"]):
                            src = probs[:, i % 2, c0:c0 + nk] if masked else ps[:, i % 2, c0:c0 + nk]
                            ins = nc.scalar.activation(probs[:, i % 2, c0:c0 + nk], src, ACT.Exp,
                                                       bias=nmx[:, i % 2, r:r + 1], scale=it["scale"],
                                                       accum_out=psums[:, i % 2, r:r + 1])
                        ins.then_inc(s["exp_done"].sem, 1)
                    m = mod_chunk(name, i)
                    if m is not None:
                        ms = st[name + "_mod"]
                        act.wait_ge(ms["mod_ready"].sem, ms["mod_ready"].at(m + 1))
                        if m >= 1:
                            act.wait_ge(ms["mod_summed"].sem, ms["mod_summed"].at(m))
                        nc.scalar.copy(mod_rows, ps[:, 6, :].rearrange("p (a b) -> p a b", a=2))\
                            .then_inc(ms["mod_copied"].sem, 1)
                    j = i - 1
                    if 0 <= j < n:
                        act.wait_ge(s["probsT_ready"].sem, s["probsT_ready"].at(j + 1))
                        if j >= 2:
                            act.wait_ge(s["out_ready"].sem, s["out_ready"].at(j - 1))
                        tiles = [t for t, _ in items[j]["pv"]]
                        src = ps[:, 2 + j % 2, :].rearrange("p (a b) -> p a b", a=4)
                        if tiles == [0, 2]:
                            dst, src = probsT[:, j % 2, 0:4:2, :], src[:, 0:4:2, :]
                        else:
                            dst, src = probsT[:, j % 2, 0:len(tiles), :], src[:, 0:len(tiles), :]
                        nc.scalar.copy(dst, src).then_inc(s["probsT_done"].sem, 1)
                    j = i - 2
                    if 0 <= j < n and items[j]["last"]:
                        it = items[j]
                        act.wait_ge(s["out_ready"].sem, s["out_ready"].at(j + 1))
                        o = outs[j]
                        nc.scalar.copy(it["dst"], ps[:, 4 + o % 2, 0:P]).then_inc(s["out_done"].sem, 1)

            def ffn(name):
                s = st[name]

                def copy(t, par, first):
                    act.wait_ge(s["up_ready"].sem, s["up_ready"].at(t + 1))
                    if not first:
                        act.wait_ge(s["conv_b"].sem, s["conv_b"].at(t - 1))
                    nc.scalar.copy(U[:, par, :, 2:S + 2], ps[:, par, :].rearrange("p (a b) -> p a b", a=2))\
                        .then_inc(s["up_copied"].sem, 1)

                def silu(t, par, first):
                    act.wait_ge(s["conv_a"].sem, s["conv_a"].at(t + 1))
                    if not first:
                        act.wait_ge(s["gated"].sem, s["gated"].at(t - 1))
                    nc.scalar.activation(sg[:, par, :], conv_ab[:, par, 0, :], ACT.Silu)\
                        .then_inc(s["silu_done"].sem, 1)

                def tile(t, par, first=False):
                    copy(t, par, first)
                    silu(t, par, first)

                tile(0, 0, True)
                tile(1, 1, True)
                whole = (FT - 2) // RING
                with act.Fori(0, whole) as i:
                    for u in range(RING):
                        tile(i * RING + (2 + u), u % 2)
                for t in range(2 + whole * RING, FT):
                    tile(t, t % 2)

            def gate_rows(name, streams):
                s = st[name]
                for i in range(2 * streams):
                    act.wait_ge(s["banks_ready"].sem, s["banks_ready"].at(i + 1))
                    nc.scalar.copy(gb[:, i // 2, (i % 2) * BW:(i % 2 + 1) * BW], ps[:, i, :])\
                        .then_inc(s["act_evac"].sem, 1)

            def experts(name, T):
                s = st[name]
                nb = n_pairs(T * P)
                y_stored = [s["y_stored0"], s["y_stored1"]]

                def silu(b, par):
                    act.wait_ge(s["gate_ready"].sem, s["gate_ready"].at(b + 1))
                    nc.scalar.activation(sgm[:, par, :], ps[:, 2, :], ACT.Silu).then_inc(s["gate_silu"].sem, 1)

                def rows_out_(b, i, par, first=False):
                    if not first:
                        act.wait_ge(y_stored[par].sem, i * 16 + y_stored[par].base)
                    for h in range(2):
                        act.wait_ge(s["down_ready"].sem, s["down_ready"].at(b * 2 + (h + 1)))
                        nc.scalar.copy(ym[:, par, h * BW:(h + 1) * BW], ps[:, 5 + h, :]).then_inc(s["down_done"].sem, 1)
                    act.wait_ge(s["down_done"].sem, s["down_done"].at(b * 2 + 2))
                    act.dma_start(y_rows[bass.ds(b * P, P), :], ym[:, par, :]).then_inc(y_stored[par].sem, 16)

                def two(i, first):
                    for u in range(2):
                        silu(i * 2 + u, u)
                        rows_out_(i * 2 + u, i, u, first)

                two(0, True)
                with act.Fori(1, nb // 2) as i:
                    two(i, False)
                silu(nb - 1, 0)
                rows_out_(nb - 1, nb // 2, 0)

            def route(name, T):
                s = st[name]
                act.wait_ge(s["route_dve"].sem, s["route_dve"].at(1))
                nc.scalar.activation(g4["e"][:, 0:T, :], g4["a"][:, 0:T, :], ACT.Exp).then_inc(s["route_act"].sem, 1)
                act.wait_ge(s["route_dve"].sem, s["route_dve"].at(2))
                nc.scalar.activation(e8["e"][:, 0:T, :], e8["t"][:, 0:T, :], ACT.Exp).then_inc(s["route_act"].sem, 1)

            act.wait_ge(const_loaded, CONST_LOADS * 16)
            nc.scalar.activation(small["ccol"][:], small["ccol"][:], ACT.Silu).then_inc(st["mod"]["route_act"].sem, 1)
            act.wait_ge(x_loaded, 16)
            norm("normA0", lat, TC)
            after(act, "normA0")
            evac("projA", 4 * TC)
            after(act, "projA")
            act.wait_ge(mem_loaded, 16)
            norm("normM0", mem_rows, TC)
            after(act, "normM0")
            evac("mem0", TC)
            s = st["ropeA"]
            act.wait_ge(s["dve_evac"].sem, s["dve_evac"].at(1))
            nc.scalar.activation(gates.rearrange("p a b c -> p (a b c)"), gates.rearrange("p a b c -> p (a b c)"),
                                 ACT.Sigmoid).then_inc(s["act_evac"].sem, 1)
            after(act, "mem0", "ropeA")
            evac("headsA", 56 // 4)
            s = st["cmp1"]
            after(act, "headsA")
            for kind in range(2):
                act.wait_ge(s["banks_ready"].sem, s["banks_ready"].at(kind + 3))
                for t in range(2):
                    ins = nc.scalar.activation(hid[:, kind, t, :], ps[:, 2 * kind + t, 0:NG * N_CMP],
                                               ACT.Gelu_apprx_tanh, bias=b1c[:, kind, t:t + 1])
                ins.then_inc(s["act_evac"].sem, 1)
            s = st["cmpatt"]
            for c in range(TC):
                act.wait_ge(s["cmp_sub"].sem, s["cmp_sub"].at(c + 1))
                x = pcmp[:, c, :, :]
                nc.scalar.activation(x, x, ACT.Exp).then_inc(s["cmp_exp"].sem, 1)
            after(act, "cmpatt")
            attention("nsa")
            after(act, "nsa", "nsa_mod")
            after(act, "wo0")
            norm("normF0", lat, TC)
            after(act, "normF0")
            ffn("ffn0")
            after(act, "ffn0")
            norm("normA1", lat, TC)
            after(act, "normA1")
            evac("b_in", 2 * TC)
            after(act, "b_in")
            norm("normS", lat, TC)
            after(act, "normS")
            evac("shared", 4 * TC)
            after(act, "shared")
            norm("normM1", mem_rows, TC)
            after(act, "normM1")
            evac("mem1", TC)
            s = st["dcum"]
            act.wait_ge(s["dve_evac"].sem, s["dve_evac"].at(1))
            nc.scalar.activation(sgf, sgf, ACT.Exp).then_inc(s["act_evac"].sem, 1)
            act.wait_ge(s["act_evac"].sem, s["act_evac"].at(1))
            nc.scalar.activation(sgf, sgf, ACT.Ln, bias=1.0).then_inc(s["act_evac"].sem, 1)
            after(act, "mem1", "dcum")
            evac("headsB", 16)
            after(act, "headsB")
            attention("fgt")
            after(act, "fgt", "fgt_mod", "wo1")
            norm("normF1", lat, TC)
            after(act, "normF1")
            ffn("ffn1")
            after(act, "ffn1")
            closing_norm("end1")
            after(act, "end1")
            act.wait_ge(ctx_loaded, 16)
            norm("normX0", both, 4)
            after(act, "normX0")
            evac("mlaN", 8)
            after(act, "mlaN", "kpe")
            evac("kpeT", 1)
            after(act, "kpeT")
            norm("normQ", lambda c: cqN[:, c, :], 4, QL)
            after(act, "normQ")
            norm("normKV", lambda c: ckvN[:, c, 0:KVL], 4, KVL)
            after(act, "normKV")
            evac("qn", MH)
            after(act, "qn")
            evac("qp", 4)
            after(act, "qp", "qrope")
            evac("qpT", MH)
            after(act, "qpT")
            evac("ukv", MH + 8)
            after(act, "ukv")
            attention("mla")
            after(act, "mla")
            gate_rows("g1_0", 1)
            after(act, "g1_0", "mla_o")

            def moe(T, norm_name, x, tag):
                norm(norm_name, x, T)
                after(act, norm_name)
                s = st["frows" + tag]
                evac("frows" + tag, 2 * T)
                for c in range(T):
                    act.wait_ge(s["act_evac"].sem, s["act_evac"].at(c + 1))
                    act.wait_ge(s["dve_evac"].sem, s["dve_evac"].at(c + 1))
                    act.dma_start(f_rows[c * P:(c + 1) * P, :], fN[:, c, :]).then_inc(s["f_stored"].sem, 16)
                route("route" + tag, T)
                after(act, "frows" + tag, "route" + tag)
                experts("moe" + tag, T)
                after(act, "moe" + tag)
                gate_rows("g2_" + tag, T // TC)
                after(act, "g2_" + tag, "comb" + tag)

            moe(TC, "normX1", lat, "0")
            norm("normX2", lat, TC)
            after(act, "normX2")
            s = st["conv"]
            for t in range(KT):
                act.wait_ge(s["banks_ready"].sem, s["banks_ready"].at(2 * t + 1))
                if t >= 2:
                    act.wait_ge(s["dve_evac"].sem, s["dve_evac"].at(t - 1))
                nc.scalar.copy(cbuf[:, t % 2, :, :], ps[:, (2 * t) % BANKS, :].rearrange("p (a b) -> p a b", a=2))\
                    .then_inc(s["act_evac"].sem, 1)
            after(act, "conv")
            gate_rows("g1_1", 1)
            after(act, "g1_1", "conv_o")
            moe(TC, "normX3", lat, "1")
            closing_norm("final")

        @block.vector
        def _(v):
            tt, ts, stt = nc.vector.tensor_tensor, nc.vector.tensor_scalar, nc.vector.scalar_tensor_tensor
            mult, add, sub = ALU.mult, ALU.add, ALU.subtract

            def evac(name, n):
                s = st[name]
                for i in range(1, n, 2):
                    dst, src, factor = OUT[name](i)
                    v.wait_ge(s["banks_ready"].sem, s["banks_ready"].at(i + 1))
                    ts(dst, src, factor, None, mult).then_inc(s["dve_evac"].sem, 1)

            def inverse_rms(name, T, width):
                s = st[name]
                for c in range(T):
                    v.wait_ge(s["squares_done"].sem, s["squares_done"].at(c + 1))
                    nc.vector.tensor_reduce(part_sums[:, c, 0:width // 32],
                                            squares(c, width).rearrange("p (a b) -> p a b", b=32), AX.X, add)\
                        .then_inc(s["squares_summed"].sem, 1)
                v.wait_ge(s["squares_summed"].sem, s["squares_summed"].end)
                link(v, nc.vector.tensor_reduce(sums[:, 0:T], part_sums[:, 0:T, 0:width // 32], AX.X, add))
                link(v, ts(var[:, 0:T], sums[:, 0:T], 1.0 / width, EPS, mult, add))
                nc.vector.reciprocal(rvar[:, 0:T], var[:, 0:T]).then_inc(s["rvar_done"].sem, 1)
                v.wait_ge(s["rstd_done"].sem, s["rstd_done"].end)
                r, t = rstd[:, 0:T], rvar[:, 0:T]
                link(v, tt(t, r, r, mult))
                link(v, tt(t, t, var[:, 0:T], mult))
                link(v, ts(t, t, -0.5, 1.5, mult, add))
                link(v, tt(r, r, t, mult))

            def norm(name, x, T, gain, width=D, shift=None, dst=hT):
                s = st[name]
                if s["rstd_done"].n:
                    inverse_rms(name, T, width)
                per, kk = max(1, width // BW), min(4, width // P)

                def scale(c):
                    ts(xh[:, c % 2, 0:width], x(c), rstd[:, c:c + 1], None, mult).then_inc(s["rows_scaled"].sem, 1)

                scale(0)
                for c in range(T):
                    if c + 1 < T:
                        if c >= 1:
                            v.wait_ge(s["banks_ready"].sem, s["banks_ready"].at(per * c))
                        scale(c + 1)
                    for h in range(per):
                        i = c * per + h
                        v.wait_ge(s["banks_ready"].sem, s["banks_ready"].at(i + 1))
                        out = dst[:, 4 * h:4 * h + kk, c * P:(c + 1) * P]
                        src = ps[:, i % 4, 0:kk * P].rearrange("p (a b) -> p a b", a=kk)

                        def wide(g):
                            return g[:, 4 * h:4 * h + kk].unsqueeze(2).broadcast_to([P, kk, P])
                        if shift is None:
                            tt(out, src, wide(gain(c)), mult).then_inc(s["dve_evac"].sem, 1)
                        else:
                            link(v, tt(out, src, wide(gain(c)), mult))
                            tt(out, out, wide(shift(c)), add).then_inc(s["dve_evac"].sem, 1)

            def closing_norm(name):
                s = st[name]
                inverse_rms(name, TC, D)
                v.wait_ge(s["aux_loaded"].sem, s["aux_loaded"].end)
                for c in range(TC):
                    link(v, ts(x_res[:, c, :], x_res[:, c, :], rstd[:, c:c + 1], None, mult))
                    tt(x_res[:, c, :], x_res[:, c, :], fg_row, mult).then_inc(s["rows_scaled"].sem, 1)

            def gcol(i):
                return lambda c: small["gcols"][:].rearrange("p (i k) -> p i k", k=KT)[:, i, :]

            def mod_part(layer, part, c):
                return mod[:, layer, part * KT:(part + 1) * KT, 0 if c < TC else 1]

            def mod_norm(name, x, T, layer, which):
                g = small["modg"][:].rearrange("p (w l k) -> p w l k", w=2, l=DEPTH)[:, which, layer, :]
                scale = mod[:, layer, (3 * which + 1) * KT:(3 * which + 2) * KT, :]
                link(v, ts(gs[:], scale, 1.0, None, add))
                link(v, tt(gs[:], gs[:], g.unsqueeze(2).broadcast_to([P, KT, 2]), mult))
                norm(name, x, T, lambda c: gs[:, :, 0 if c < TC else 1],
                     shift=lambda c: mod_part(layer, 3 * which, c))

            def attention(name):
                s, items = st[name], ATT[name]
                n = len(items)
                if MOD_OF[name] is not None:
                    ms = st[name + "_mod"]
                    nc.vector.memset(ps[:, 6, :], 0.0).then_inc(ms["mod_zeroed"].sem, 1)
                for i in range(n + 1):
                    if i < n:
                        it = items[i]
                        v.wait_ge(s["scores_ready"].sem, s["scores_ready"].at(i + 1))
                        if i >= 2:
                            v.wait_ge(s["probsT_ready"].sem, s["probsT_ready"].at(i - 1))
                        R = len(it["regions"])
                        for r, (c0, nk, masked, _) in enumerate(it["regions"]):
                            src = ps[:, i % 2, c0:c0 + nk]
                            if masked:
                                ins = nc.vector.tensor_tensor_reduce(
                                    out=probs[:, i % 2, c0:c0 + nk], in0=src, in1=const["causal"][:, 2 * P - nk:2 * P],
                                    scale=1.0, scalar=-3.0e38, op0=add, op1=ALU.max,
                                    accum_out=mx[:, i % 2, r:r + 1])
                            else:
                                ins = nc.vector.tensor_reduce(mx[:, i % 2, r:r + 1], src, AX.X, ALU.max)
                        link(v, ins)
                        ts(nmx[:, i % 2, 0:R], mx[:, i % 2, 0:R], -it["scale"], None, mult)\
                            .then_inc(s["max_done"].sem, 1)
                    j = i - 1
                    if j >= 0:
                        it = items[j]
                        R = len(it["regions"])
                        v.wait_ge(s["exp_done"].sem, s["exp_done"].at(j + 1))
                        link(v, nc.vector.reciprocal(pinv[:, j % 2, 0:R], psums[:, j % 2, 0:R]))
                        for r, (c0, nk, _, gate) in enumerate(it["regions"]):
                            p = probs[:, j % 2, c0:c0 + nk]
                            if gate is None:
                                ins = ts(p, p, pinv[:, j % 2, r:r + 1], None, mult)
                            else:
                                ins = ts(p, p, pinv[:, j % 2, r:r + 1], gate, mult, mult)
                        ins.then_inc(s["probs_done"].sem, 1)
                if MOD_OF[name] is not None:
                    l = MOD_OF[name]
                    v.wait_ge(ms["mod_summed"].sem, ms["mod_summed"].end)
                    tt(mod[:, l, :, :], ps[:, 7, 0:2 * N_MOD * KT].rearrange("p (k s) -> p k s", s=2),
                       bmod[:, l, :].unsqueeze(2).broadcast_to([P, N_MOD * KT, 2]), add)\
                        .then_inc(ms["dve_evac"].sem, 1)

            def rope(x1, x2, cos, sin, tmp):
                a, b, c, d = tmp
                tt(a, x1, cos, mult)
                tt(b, x2, sin, mult)
                tt(c, x2, cos, mult)
                link(v, tt(d, x1, sin, mult))
                tt(x1, a, b, sub)
                return tt(x2, c, d, add)

            def residual(name, T, x, gated):
                s = st[name]
                for i in range(2 * T):
                    half, c = i // T, i % T
                    out = x(c)[:, half * BW:(half + 1) * BW]
                    v.wait_ge(s["banks_ready"].sem, s["banks_ready"].at(i + 1))
                    if gated:
                        link(v, tt(prod[:, i % 2, :], ps[:, i % BANKS, :],
                                   gb[:, c // TC, half * BW:(half + 1) * BW], mult))
                        tt(out, out, prod[:, i % 2, :], add).then_inc(s["dve_evac"].sem, 1)
                    else:
                        tt(out, out, ps[:, i % BANKS, :], add).then_inc(s["dve_evac"].sem, 1)

            def ffn(name):
                s = st[name]
                n0 = first_of(name)
                v.wait_ge(s["aux_loaded"].sem, s["aux_loaded"].end)
                nc.vector.memset(U[:, :, 0, 0:2], 0.0)
                link(v, nc.vector.memset(U[:, :, 1, 0:2], 0.0))

                def conv(t, par, first):
                    v.wait_ge(s["up_copied"].sem, s["up_copied"].at(t + 1))
                    if not first:
                        v.wait_ge(s["gated"].sem, s["gated"].at(t - 1))
                    w = lambda tap, f: convw[:, tap, bass.ds(t + f * FT, 1)]
                    for f in range(2):
                        ts(conv_ab[:, par, f, :], U[:, par, f, 0:S], w(0, f), w(3, f), mult, add)\
                            .then_inc(s["conv_step"].sem, 1)
                    for f in range(2):
                        v.wait_ge(s["conv_step"].sem, s["conv_step"].at(t * 4 + (f + 1)))
                        stt(conv_ab[:, par, f, :], U[:, par, f, 1:S + 1], w(1, f), conv_ab[:, par, f, :], mult, add)\
                            .then_inc(s["conv_step"].sem, 1)
                    for f in range(2):
                        v.wait_ge(s["conv_step"].sem, s["conv_step"].at(t * 4 + (f + 3)))
                        stt(conv_ab[:, par, f, :], U[:, par, f, 2:S + 2], w(2, f), conv_ab[:, par, f, :], mult, add)\
                            .then_inc((s["conv_b"] if f else s["conv_a"]).sem, 1)

                def gate(t, par, first):
                    v.wait_ge(s["silu_done"].sem, s["silu_done"].at(t + 1))
                    v.wait_ge(s["conv_b"].sem, s["conv_b"].at(t + 1))
                    if not first:
                        v.wait_ge(chunk_used, t + (n0 - 1))
                    tt(gT[:, par, :], sg[:, par, :], conv_ab[:, par, 1, :], mult).then_inc(s["gated"].sem, 1)

                def tile(t, par, first=False):
                    conv(t, par, first)
                    gate(t, par, first)

                tile(0, 0, True)
                tile(1, 1, True)
                whole = (FT - 2) // RING
                with v.Fori(0, whole) as i:
                    for u in range(RING):
                        tile(i * RING + (2 + u), u % 2)
                for t in range(2 + whole * RING, FT):
                    tile(t, t % 2)
                v.wait_ge(s["banks_ready"].sem, s["banks_ready"].end)
                for c in range(TC):
                    for h in range(2):
                        out = x_res[:, c, h * BW:(h + 1) * BW]
                        ins = tt(out, out, ps[:, 4 + 2 * c + h, :], add)
                ins.then_inc(s["dve_evac"].sem, 1)

            def gate_rows(name, streams, layer, part):
                s = st[name]
                for r in range(streams):
                    if r:
                        v.wait_ge(s["banks_ready"].sem, s["banks_ready"].at(2 * r))
                    tt(diag, const["ident"][:].unsqueeze(1).broadcast_to([P, KT, P]),
                       mod[:, layer, part * KT:(part + 1) * KT, r].unsqueeze(2).broadcast_to([P, KT, P]), mult)\
                        .then_inc(s["diag_done"].sem, 1)

            def route(name, T):
                s = st[name]
                sv = lambda n: t1[n][:, 0:T]
                col = lambda n, w: t1[n][:, 0:T].unsqueeze(2).broadcast_to([P, T, w])
                g, e = {n: a[:, 0:T, :] for n, a in g4.items()}, {n: a[:, 0:T, :] for n, a in e8.items()}
                gl, el = lg[:, 0:T, 0:G], lg[:, 0:T, G:G + E].rearrange("p t (g e) -> p t g e", g=G)
                iota = lambda w: const["iota"][:, 0:w].unsqueeze(1).broadcast_to([P, T, w])
                red = lambda out, src, op: link(v, nc.vector.tensor_reduce(out, src, AX.X, op))
                L = lambda ins: link(v, ins)

                def first_max(score, eq, idx, onehot, w, m):
                    red(sv(m), score, ALU.max)
                    L(tt(eq, score, col(m, w), ALU.is_equal))
                    L(stt(eq, eq, -64.0, iota(w), mult, add))
                    red(sv(idx), eq, ALU.min)
                    L(ts(sv(idx), sv(idx), 64.0, None, add))
                    L(tt(onehot, iota(w), col(idx, w), ALU.is_equal))

                v.wait_ge(s["route_pe"].sem, s["route_pe"].at(1))
                L(nc.vector.tensor_copy(lg[:, 0:T, :], ps[:, 0, 0:T * (G + E)].rearrange("p (t n) -> p t n", t=T)))
                red(sv("m"), gl, ALU.max)
                tt(g["a"], gl, col("m", G), sub).then_inc(s["route_dve"].sem, 1)
                v.wait_ge(s["route_act"].sem, s["route_act"].at(1))
                red(sv("s"), g["e"], add)
                L(nc.vector.reciprocal(sv("r"), sv("s")))
                L(tt(g["p"], g["e"], col("r", G), mult))
                v.wait_ge(s["aux_loaded"].sem, s["aux_loaded"].end)
                L(tt(g["b"], g["p"], bg_r.unsqueeze(1).broadcast_to([P, T, G]), add))
                first_max(g["b"], g["eq"], "gi", g["oh"], G, "m")
                L(tt(g["eq"], g["oh"], g["p"], mult))
                red(sv("gw"), g["eq"], add)
                prod4 = t32["prod"][:, 0:T]
                by_e = prod4.rearrange("p t g e -> p t e g")
                for t in range(T):
                    oh = g["oh"][:, t, :].unsqueeze(2).broadcast_to([P, G, EPG])
                    ins = tt(prod4[:, t], el[:, t], oh, mult)
                L(ins)
                red(e["el"], by_e, add)
                for t in range(T):
                    oh = g["oh"][:, t, :].unsqueeze(2).broadcast_to([P, G, EPG])
                    ins = tt(prod4[:, t], be_r, oh, mult)
                L(ins)
                red(e["b"], by_e, add)
                red(sv("m2"), e["el"], ALU.max)
                tt(e["t"], e["el"], col("m2", EPG), sub).then_inc(s["route_dve"].sem, 1)
                v.wait_ge(s["route_act"].sem, s["route_act"].at(2))
                red(sv("s2"), e["e"], add)
                L(nc.vector.reciprocal(sv("r2"), sv("s2")))
                L(tt(e["p"], e["e"], col("r2", EPG), mult))
                L(tt(e["sc"], e["p"], e["b"], add))
                for k in range(2):
                    o = f"o{k}"
                    first_max(e["sc"], e["eq"], f"i{k}", e[o], EPG, "m")
                    L(tt(e["t"], e[o], e["p"], mult))
                    red(sv(f"w{k}"), e["t"], add)
                    if k == 0:
                        L(stt(e["sc"], e[o], NEG, e["sc"], mult, add))
                L(tt(sv("ws"), sv("w0"), sv("w1"), add))
                L(nc.vector.reciprocal(sv("wr"), sv("ws")))
                L(tt(sv("wr"), sv("wr"), sv("gw"), mult))
                for k in range(2):
                    tt(wts[:, k, 0:T], sv(f"w{k}"), sv("wr"), mult)
                    for t in range(T):
                        ins = tt(t32[f"E{k}"][:, t], g["oh"][:, t, :].unsqueeze(2).broadcast_to([P, G, EPG]),
                                 e[f"o{k}"][:, t, :].unsqueeze(1).broadcast_to([P, G, EPG]), mult)
                    L(ins)
                flat = lambda n: t32[n][:, 0:T].rearrange("p t g e -> p t (g e)")
                tt(flat("M"), flat("E0"), flat("E1"), add).then_inc(s["route_dve"].sem, 1)
                v.wait_ge(s["route_pe"].sem, s["route_pe"].at(2))
                L(ts(nbT[0:E, :], ps[0:E, 2, 0:P], float(SLOTS + 1), 1.0, ALU.is_ge, add))
                for j in range(2, T * P // SLOTS):
                    ins = stt(nbT[0:E, :], ps[0:E, 2, 0:P], float(j * SLOTS + 1), nbT[0:E, :], ALU.is_ge, add)
                    if j < T * P // SLOTS - 1:
                        L(ins)
                ins.then_inc(s["route_dve"].sem, 1)
                v.wait_ge(s["route_pe"].sem, s["route_pe"].at(3))
                tt(nbm[0:E, :], nbT[0:E, :], ps[0:E, 7, 0:P], ALU.max).then_inc(s["route_dve"].sem, 1)
                v.wait_ge(s["route_pe"].sem, s["route_pe"].at(4))
                nc.vector.memset(pad_f[:, E:E + 1], 0.0)
                ts(rest[:, 0:E], ps[:, 3, E:2 * E], -1.0, float(n_pairs(T * P)), mult, add)
                L(ts(rest[0:E, E:E + 1], ps[0:E, 4, 1:2], -1.0, float(n_pairs(T * P)), mult, add))
                tt(pad_f[:, 0:E], rest[:, 0:E], rt[:, 2, :], mult)
                L(tt(pad_f[0:E, E:E + 1], rest[0:E, E:E + 1], rt[0:E, 4, 0:1], mult))
                L(nc.vector.tensor_copy(pad_i, pad_f))
                L(ts(pad_i, pad_i, GR.bit_length() - 1, None, ALU.logical_shift_right))
                L(nc.vector.tensor_copy(pad_f, pad_i))
                L(tt(pst, ps[:, 3, 0:E], pad_f[:, 0:E], add))
                L(tt(pend[0:E, :], ps[0:E, 4, 0:1], pad_f[0:E, E:E + 1], add))
                ts(past[0:E, :], const["iota"][0:E, 0:NPAIR], pend[0:E, :], None, ALU.is_ge)\
                    .then_inc(s["route_dve"].sem, 1)
                L(nc.vector.tensor_copy(need_i, pst[0:1, :]))
                L(stt(pst, pst, float(P), rt[:, 3, :], mult, add))
                before = ps[:, 1, 0:T * E].rearrange("p (t n) -> p t n", t=T)
                for k in range(2):
                    L(tt(flat("prod"), flat(f"E{k}"), before, mult))
                    red(rk[:, k, 0:T], flat("prod"), add)
                    L(tt(flat("prod"), flat(f"E{k}"), pst.unsqueeze(1).broadcast_to([P, T, E]), mult))
                    red(dst_f[:, k, 0:T], flat("prod"), add)
                L(nc.vector.tensor_copy(rk_i[:, :, 0:T], rk[:, :, 0:T]))
                L(ts(rk_i[:, :, 0:T], rk_i[:, :, 0:T], SLOTS.bit_length() - 1, None, ALU.logical_shift_right))
                L(nc.vector.tensor_copy(rk_f[:, :, 0:T], rk_i[:, :, 0:T]))
                L(tt(dst_f[:, :, 0:T], dst_f[:, :, 0:T], rk[:, :, 0:T], add))
                L(stt(dst_f[:, :, 0:T], rk_f[:, :, 0:T], float(SLOTS), dst_f[:, :, 0:T], mult, add))
                L(nc.vector.tensor_copy(dest_i[:, :, 0:T], dst_f[:, :, 0:T]))
                ts(q_i[:, :, 0:T], dest_i[:, :, 0:T], P - 1, None, ALU.bitwise_and)
                L(ts(b_i[:, :, 0:T], dest_i[:, :, 0:T], P.bit_length() - 1, None, ALU.logical_shift_right))
                nc.vector.tensor_copy(q_f[:, :, 0:T], q_i[:, :, 0:T])
                L(nc.vector.tensor_copy(b_f[:, :, 0:T], b_i[:, :, 0:T]))
                for r in range(2 * T):
                    k, c = r // T, r % T
                    if r >= 2:
                        v.wait_ge(s["route_pe"].sem, s["route_pe"].at(5 + r - 1))
                    ts(onA[:, r % 2, :], const["iota"][:], q_f[:, k, c:c + 1], None, ALU.is_equal)
                    ts(onB[:, r % 2, :], const["iota"][:, 0:NPAIR], b_f[:, k, c:c + 1], const["tokid"][:, c:c + 1],
                       ALU.is_equal, mult).then_inc(s["route_dve"].sem, 1)
                v.wait_ge(s["route_pe"].sem, s["route_pe"].end)
                L(ts(past[0:1, :], ps[0:1, 5, 0:NPAIR], 16.0, 16.0, mult, add))
                L(nc.vector.tensor_copy(tab_i, past[0:1, :]))
                nc.vector.tensor_copy(slot_i, ps[:, 6, 0:NPAIR]).then_inc(s["route_dve"].sem, 1)

            def experts(name, T):
                s = st[name]
                nb = n_pairs(T * P)

                def rows_T(b, par):
                    for h in range(2):
                        v.wait_ge(s["xT_ready"].sem, s["xT_ready"].at(b * 2 + (h + 1)))
                        nc.vector.tensor_copy(xeT[:, par, 4 * h:4 * h + 4, :],
                                              ps[:, h, :].rearrange("p (a b) -> p a b", a=4))\
                            .then_inc(s["xT_done"].sem, 1)

                def hidden(b, par):
                    v.wait_ge(s["gate_silu"].sem, s["gate_silu"].at(b + 1))
                    v.wait_ge(s["upm_ready"].sem, s["upm_ready"].at(b + 1))
                    tt(hm[:, par, :], sgm[:, par, :], ps[:, 3, :], mult).then_inc(s["hidden_done"].sem, 1)

                def hidden_T(b, par):
                    v.wait_ge(s["hT_ready"].sem, s["hT_ready"].at(b + 1))
                    nc.vector.tensor_copy(hmT[:, par, :, :], ps[:, 4, :].rearrange("p (a b) -> p a b", a=4))\
                        .then_inc(s["hT_done"].sem, 1)

                rows_T(0, 0)

                def pair(b, par):
                    hidden(b, par)
                    rows_T(b + 1, 1 - par)
                    hidden_T(b, par)

                with v.Fori(0, nb // 2) as i:
                    for u in range(2):
                        pair(i * 2 + u, u)
                hidden(nb - 1, 0)
                hidden_T(nb - 1, 0)

            def combine(name, T, x):
                s = st[name]
                fetched = [s["y_fetched0"], s["y_fetched1"]]
                for c in range(T):
                    y0, y1 = y01[:, c % 2, 0, :], y01[:, c % 2, 1, :]
                    v.wait_ge(fetched[c % 2].sem, fetched[c % 2].at(32 * (c // 2 + 1)))
                    link(v, ts(y0, y0, wts[:, 0, c:c + 1], None, mult))
                    link(v, stt(y0, y1, wts[:, 1, c:c + 1], y0, mult, add))
                    link(v, tt(y0, y0, gb[:, c // TC, :], mult))
                    tt(x(c), x(c), y0, add).then_inc(s["combined"].sem, 1)

            v.wait_ge(const_loaded, CONST_LOADS * 16)
            v.wait_ge(x_loaded, 16)
            norm("normA0", lat, TC, gcol(0))
            after(v, "normA0")
            evac("projA", 4 * TC)
            after(v, "projA")
            v.wait_ge(mem_loaded, 16)
            norm("normM0", mem_rows, TC, gcol(4))
            after(v, "normM0")
            evac("mem0", TC)
            after(v, "mem0")
            s = st["ropeA"]
            for c in range(TC):
                ins = tt(gates[:, c].rearrange("p a b -> p (a b)"), projA[:, c, GATE0:GATE0 + GATE_W], gate_br, add)
            ins.then_inc(s["dve_evac"].sem, 1)
            for c in range(TC):
                q = projA[:, c, 0:MIX_W].rearrange("p (h f x) -> p h f x", h=NH, f=2)
                cs = lambda i: ropeT[:, c, i, :].unsqueeze(1).broadcast_to([P, NH, 32])
                link(v, rope(q[:, :, 0, :], q[:, :, 1, :], cs(0), cs(1),
                             [rtmp4[:, i, :].rearrange("p (h x) -> p h x", h=NH) for i in range(4)]))
                for b in range(2):
                    k0 = KV0 + (2 + 2 * b) * NG * HD
                    k = projA[:, c, k0:k0 + NG * HD].rearrange("p (h f x) -> p h f x", h=NG, f=2)
                    cs = lambda i: ropeT[:, c, i, :].unsqueeze(1).broadcast_to([P, NG, 32])
                    ins = rope(k[:, :, 0, :], k[:, :, 1, :], cs(0), cs(1),
                               [rtmp4[:, i, 0:NG * 32].rearrange("p (h x) -> p h x", h=NG) for i in range(4)])
                    if (c, b) != (TC - 1, 1):
                        link(v, ins)
            ins.then_inc(s["dve_evac"].sem, 1)
            after(v, "ropeA")
            evac("headsA", 56 // 4)
            after(v, "headsA")
            s = st["cmp1"]
            nc.vector.memset(ps[:, 4:6, 0:CMP_HID], 0.0)
            for kind in range(2):
                u = headsT[:, B_CK + 4 * kind:B_CK + 4 * kind + 4, :].rearrange("p (g c) (m b) -> p g (c m) b", g=NG, b=16)
                for a in range(2):
                    for g in range(NG):
                        out = windows[:, kind, 16 * a:16 * a + 16, g * N_CMP:(g + 1) * N_CMP].rearrange("p b n -> p n b")
                        ins = tt(out, u[:, g, a:a + N_CMP, :],
                                 posT[:, kind, 16 * a:16 * a + 16].unsqueeze(1).broadcast_to([HD, N_CMP, 16]), add)
            ins.then_inc(s["dve_evac"].sem, 1)
            for kind in range(2):
                v.wait_ge(s["banks_ready"].sem, s["banks_ready"].at(kind + 1))
                nc.vector.tensor_copy(mod_rows[:, kind, :], ps[:, 4 + kind, 0:CMP_HID]).then_inc(s["dve_evac"].sem, 1)
            after(v, "cmp1")
            s = st["cmp2"]
            n = NG * N_CMP
            v.wait_ge(s["banks_ready"].sem, s["banks_ready"].at(1))
            link(v, tt(kcN[0:n, :], ps[0:n, 4, 0:HD], b2r[0:n, 0, :], add))
            kc = kcN[0:n, :].rearrange("p (f x) -> p f x", f=2)
            rope(kc[:, 0, :], kc[:, 1, :], rope_cmp[0:n, 0, :], rope_cmp[0:n, 1, :],
                 [rtmp4[0:n, i, 0:32] for i in range(4)]).then_inc(s["dve_evac"].sem, 1)
            for g in range(NG):
                v.wait_ge(s["banks_ready"].sem, s["banks_ready"].at(2 + g))
                tt(vcN[0:N_CMP, g, :], ps[0:N_CMP, 5 + g, 0:HD], b2r[0:N_CMP, 1, :], add).then_inc(s["dve_evac"].sem, 1)
            v.wait_ge(s["banks_ready"].sem, s["banks_ready"].at(4))
            nc.vector.tensor_copy(kcT[0:HD, :], ps[0:HD, 7, 0:n]).then_inc(s["dve_evac"].sem, 1)
            s = st["cmpatt"]
            after(v, "cmp2")
            row = lambda a: a.unsqueeze(1).broadcast_to([P, NH, N_CMP])
            per_head = lambda a: a.unsqueeze(2).broadcast_to([P, NH, N_CMP])
            for c in range(TC):
                pc, m, w = pcmp[:, c, :, :], cst[:, c, :, 0], cst[:, c, :, 1]
                v.wait_ge(s["cmp_ready"].sem, s["cmp_ready"].at(c + 1))
                link(v, tt(pc, ps[:, c, 0:NH * N_CMP].rearrange("p (h n) -> p h n", h=NH), row(cmp_bias[:, c, :]), add))
                link(v, nc.vector.tensor_reduce(m, pc, AX.X, ALU.max))
                tt(pc, pc, per_head(m), sub).then_inc(s["cmp_sub"].sem, 1)
                v.wait_ge(s["cmp_exp"].sem, s["cmp_exp"].at(c + 1))
                link(v, tt(pc, pc, row(cmp_seen[:, c, :]), mult))
                link(v, nc.vector.tensor_reduce(m, pc, AX.X, add))
                link(v, ts(m, m, 1e-30, None, ALU.max))
                link(v, nc.vector.reciprocal(w, m))
                link(v, tt(w, w, gates[:, c, :, 0], mult))
                tt(pc, pc, per_head(w), mult).then_inc(s["cmp_probs"].sem, 1)
            for i in range(3 * TC):
                c, q = i // 3, i % 3
                v.wait_ge(s["cmpT_ready"].sem, s["cmpT_ready"].at(i + 1))
                nc.vector.tensor_copy(pcT[0:N_CMP, 4 * q:4 * q + 4, c * P:(c + 1) * P],
                                      ps[0:N_CMP, 2 + i, :].rearrange("p (a b) -> p a b", a=4))\
                    .then_inc(s["cmpT_done"].sem, 1)
            after(v, "cmpatt")
            attention("nsa")
            after(v, "nsa", "nsa_mod")
            residual("wo0", TC, lat, False)
            after(v, "wo0")
            norm("normF0", lat, TC, gcol(2))
            after(v, "normF0")
            ffn("ffn0")
            after(v, "ffn0")
            norm("normA1", lat, TC, gcol(1))
            after(v, "normA1")
            evac("b_in", 2 * TC)
            after(v, "b_in")
            norm("normS", lat, TC, gcol(6))
            after(v, "normS")
            evac("shared", 4 * TC)
            after(v, "shared")
            norm("normM1", mem_rows, TC, gcol(5))
            after(v, "normM1")
            evac("mem1", TC)
            s = st["dcum"]
            for c in range(TC):
                ins = tt(logf[:, c, :], shared[:, c, 2 * MIX_W:SHARED_W], small["b_fgate"][:], add)
            link(v, ins)
            link(v, ts(sgf, logf, -1.0, None, mult))
            tt(sgf, sgf, logf, ALU.min).then_inc(s["dve_evac"].sem, 1)
            v.wait_ge(s["act_evac"].sem, s["act_evac"].at(2))
            stt(logf, logf, 0.0, sgf, ALU.min, sub).then_inc(s["dve_evac"].sem, 1)
            v.wait_ge(s["banks_ready"].sem, s["banks_ready"].end)
            ts(dcT[0:NH, :], ps[0:NH, 0, 0:2 * P], 1.0, None, mult).then_inc(s["dve_evac"].sem, 1)
            ts(ndcT[0:NH, :], ps[0:NH, 0, 0:2 * P], -1.0, None, mult).then_inc(s["dve_evac"].sem, 1)
            after(v, "mem1", "dcum")
            evac("headsB", 16)
            after(v, "headsB")
            attention("fgt")
            after(v, "fgt", "fgt_mod")
            residual("wo1", TC, lat, False)
            after(v, "wo1")
            norm("normF1", lat, TC, gcol(3))
            after(v, "normF1")
            ffn("ffn1")
            after(v, "ffn1")
            closing_norm("end1")
            after(v, "end1")
            v.wait_ge(ctx_loaded, 16)
            mod_norm("normX0", both, 4, 0, 0)
            after(v, "normX0")
            evac("mlaN", 8)
            after(v, "mlaN")
            ax = const["axial"][:].rearrange("p (c t a x) -> p c t a x", c=TC, t=2, a=2)
            for c in range(TC):
                k = ckvN[:, c, KVL:KVL + ROPE].rearrange("p (a f x) -> p a f x", a=2, f=2)
                ins = rope(k[:, :, 0, :], k[:, :, 1, :], ax[:, c, 0], ax[:, c, 1],
                           [atmp[:, i, 0:32].rearrange("p (a x) -> p a x", a=2) for i in range(4)])
                if c < TC - 1:
                    link(v, ins)
            ins.then_inc(st["kpe"]["dve_evac"].sem, 1)
            after(v, "kpe")
            evac("kpeT", 1)
            after(v, "kpeT")
            norm("normQ", lambda c: cqN[:, c, :], 4, lambda c: small["g_q"], QL, dst=cqT)
            after(v, "normQ")
            norm("normKV", lambda c: ckvN[:, c, 0:KVL], 4, lambda c: small["g_kv"], KVL, dst=ckvT)
            after(v, "normKV")
            evac("qn", MH)
            after(v, "qn")
            evac("qp", 4)
            after(v, "qp")
            for c in range(TC):
                for a in range(2):
                    q = qpN[:, c, :].rearrange("p (h a f x) -> p h a f x", h=MH, a=2, f=2)[:, :, a]
                    cs = lambda i: ax[:, c, i, a].unsqueeze(1).broadcast_to([P, MH, 16])
                    ins = rope(q[:, :, 0, :], q[:, :, 1, :], cs(0), cs(1),
                               [atmp[:, i, 0:128].rearrange("p (h x) -> p h x", h=MH) for i in range(4)])
                    if (c, a) != (TC - 1, 1):
                        link(v, ins)
            ins.then_inc(st["qrope"]["dve_evac"].sem, 1)
            after(v, "qrope")
            evac("qpT", MH)
            after(v, "qpT")
            evac("ukv", MH + 8)
            after(v, "ukv")
            attention("mla")
            after(v, "mla")
            gate_rows("g1_0", 1, 0, 2)
            after(v, "g1_0")
            residual("mla_o", TC, lat, True)
            after(v, "mla_o")

            def moe(T, norm_name, x, tag, layer):
                mod_norm(norm_name, x, T, layer, 1)
                after(v, norm_name)
                evac("frows" + tag, 2 * T)
                route("route" + tag, T)
                after(v, "frows" + tag, "route" + tag)
                experts("moe" + tag, T)
                after(v, "moe" + tag)
                gate_rows("g2_" + tag, T // TC, layer, 5)
                after(v, "g2_" + tag)
                combine("comb" + tag, T, x)
                after(v, "comb" + tag)

            moe(TC, "normX1", lat, "0", 0)
            mod_norm("normX2", lat, TC, 1, 0)
            after(v, "normX2")
            s = st["conv"]
            nc.vector.memset(cu[:, :, 0:1], 0.0)
            link(v, nc.vector.memset(cu[:, :, S + 1:S + 2], 0.0))
            for t in range(KT):
                w = lambda tap: small["conv3"][:, t * TAPS + tap:t * TAPS + tap + 1]
                v.wait_ge(s["act_evac"].sem, s["act_evac"].at(t + 1))
                v.wait_ge(s["banks_ready"].sem, s["banks_ready"].at(2 * t + 2))
                z, c_ = cz[:, t % 2, :], cu[:, t % 2, :]
                link(v, tt(c_[:, 1:S + 1], cbuf[:, t % 2, 0, :], ps[:, (2 * t + 1) % BANKS, 0:S], mult))
                link(v, ts(z, c_[:, 0:S], w(0), None, mult))
                link(v, stt(z, c_[:, 1:S + 1], w(1), z, mult, add))
                link(v, stt(z, c_[:, 2:S + 2], w(2), z, mult, add))
                tt(zT[:, t, :], z, cbuf[:, t % 2, 1, :], mult).then_inc(s["dve_evac"].sem, 1)
            after(v, "conv")
            gate_rows("g1_1", 1, 1, 2)
            after(v, "g1_1")
            residual("conv_o", TC, lat, True)
            after(v, "conv_o")
            moe(TC, "normX3", lat, "1", 1)
            closing_norm("final")

        @block.gpsimd
        def _(pool):
            def aux(name, pairs):
                s = st[name]
                for dst, src in pairs:
                    pool.dma_start(dst, src).then_inc(s["aux_loaded"].sem, 16)

            def experts(name, T):
                s = st[name]
                fetched = [s["rows_gathered0"], s["rows_gathered1"]]
                for b in range(n_pairs(T * P)):
                    if b >= 2:
                        pool.wait_ge(s["xT_ready"].sem, s["xT_ready"].at(2 * b - 2))
                    nc.gpsimd.indirect_dma_start(
                        out=xe[:, b % 2, :], out_offset=None, in_=f_rows[:, :],
                        in_offset=bass.IndirectOffsetOnAxis(ap=slot_i[:, b:b + 1], axis=0))\
                        .then_inc(fetched[b % 2].sem, 16)

            def fetch(name, T):
                s = st[name]
                fetched = [s["y_fetched0"], s["y_fetched1"]]
                for c in range(T):
                    if c >= 2:
                        pool.wait_ge(s["combined"].sem, s["combined"].at(c - 1))
                    for k in range(2):
                        nc.gpsimd.indirect_dma_start(
                            out=y01[:, c % 2, k, :], out_offset=None, in_=y_rows[:, :],
                            in_offset=bass.IndirectOffsetOnAxis(ap=dest_i[:, k, c:c + 1], axis=0))\
                            .then_inc(fetched[c % 2].sem, 16)

            after(pool, "wo0")
            aux("ffn0", [(convw, dram["convw"][0])])
            after(pool, "shared")
            aux("dcum", [(upto, dram["upto"])])
            after(pool, "wo1")
            aux("ffn1", [(convw, dram["convw"][1])])

            after(pool, "ffn1")
            aux("end1", [(fg_row, dram["first_final_g"])])

            def moe(T, before, tag, layer):
                after(pool, before)
                aux("route" + tag, [(wr, dram["w_route"][layer]), (bg_r, dram["b_group"][layer]),
                                    (be_r, dram["b_expert"][layer]), (rt, dram["router"])])
                after(pool, "frows" + tag, "route" + tag)
                experts("moe" + tag, T)
                after(pool, "moe" + tag)
                fetch("comb" + tag, T)

            moe(TC, "mla_o", "0", 0)
            moe(TC, "conv_o", "1", 1)
            after(pool, "comb1")
            aux("final", [(fg_row, dram["final_g"])])


CONSTS = ("ident", "ones", "before", "causal", "axial", "iota", "tokid")
CONST_LOADS = len(CONSTS) + len(SMALL_W) + 11 + 1


def CONST_DST(const, small, extra, selr):
    out = [(n, const[n][:]) for n in CONSTS] + [(n, small[n][:]) for n in SMALL_W]
    out += [(n, extra[n]) for n in extra]
    return out + [("sel", selr[0:NH])]


def tiles(w):
    k, n = w.shape
    return w.reshape(k // P, P, n).transpose(1, 0, 2).reshape(P, -1)


def cols(vec):
    return vec.reshape(-1, P).T


def row(vec):
    return np.broadcast_to(vec.reshape(1, -1), (P, vec.size))


def dense_chunks(i):
    def columns(w):
        for c in range(0, w.shape[1], BW):
            yield tiles(w[:, c:c + BW])

    def ffn(l):
        up, down = i["w_up"][l], i["w_down"][l]
        for t in range(FT):
            a, b = up[:, t * P:(t + 1) * P], up[:, D_FF + t * P:D_FF + (t + 1) * P]
            yield np.concatenate([tiles(np.concatenate([a, b], 1)), down[t * P:(t + 1) * P]], 1)

    yield from columns(i["a_w_in"][0])
    yield tiles(i["w_mem_kv"][0])
    for kind in range(2):
        w = i["a_cmp_w1"][0, kind].reshape(2, 16, HD, CMP_HID)
        for half in range(2):
            c = np.zeros((P, CH), np.float32)
            c[:HD] = w[half].transpose(1, 0, 2).reshape(HD, -1)
            yield c
    yield from columns(i["w_mod_2"][0])
    yield from columns(i["w_o"][0])
    yield from ffn(0)
    yield from columns(i["b_w_in"][0])
    yield from columns(i["w_kv_shared"])
    yield tiles(i["w_mem_kv"][1])
    yield from columns(i["w_mod_2"][1])
    yield from columns(i["w_o"][1])
    yield from ffn(1)
    yield tiles(i["mla_w_dq_2"][0])
    yield tiles(i["mla_w_dkv_2"][0])
    uq = i["mla_w_uq_2"][0].reshape(QL, MH, NOPE + ROPE)
    yield tiles(uq[:, :, :NOPE].reshape(QL, -1))
    yield tiles(uq[:, :, NOPE:].reshape(QL, -1))
    ukv = i["mla_w_ukv_2"][0].reshape(KVL, MH, NOPE + VD)
    yield tiles(np.concatenate([ukv[:, :, :NOPE].reshape(KVL, -1), ukv[:, :, NOPE:].reshape(KVL, -1)], 1))
    yield from columns(i["mla_w_o_2"][0])
    w = i["conv_w_in_2"][0]
    for t in range(KT):
        b, c, u = (w[:, q * D + t * P:q * D + (t + 1) * P] for q in range(3))
        yield tiles(np.concatenate([c, b, u], 1))
    yield from columns(i["conv_w_out_2"][0])


def layout(i):
    out = shape_constants()
    dense = np.zeros((len(PLAN), P, CH), np.float32)
    for r, c in enumerate(dense_chunks(i)):
        assert c.shape[1] == PLAN[r][1], (r, c.shape, PLAN[r])
        dense[r, :, :c.shape[1]] = c
    assert r == len(PLAN) - 1
    out["dense"] = dense
    out["x"], out["mem"], out["ctx"] = i["x"][0], i["mem"][0], i["ctx_2"][0]
    for name, key in (("w_gate", "moe_w_gate_2"), ("w_up", "moe_w_up_2"), ("w_down", "moe_w_down_2")):
        out[name] = i[key].reshape(DEPTH * E, P, CH)
    g = [i["attn_norm"][0], i["attn_norm"][1], i["ffn_norm"][0], i["ffn_norm"][1], i["mem_norm"][0],
         i["mem_norm"][1], i["kv_norm"]]
    out["gcols"] = np.concatenate([cols(v) for v in g], 1)
    out["modg"] = np.concatenate([cols(v) for w in ("norm_mix_g_2", "norm_ffn_g_2") for v in i[w]], 1)
    out["g_q"], out["g_kv"] = cols(i["mla_g_q_2"][0]), cols(i["mla_g_kv_2"][0])
    out["ccol"] = np.stack([cols(i["c_2"][0]), cols(i["c_ctx_2"])], 2).reshape(P, -1)
    out["conv3"] = i["conv_w_2"][0].reshape(TAPS, KT, P).transpose(2, 1, 0).reshape(P, -1)
    out["b_fgate"] = row(i["b_fgate"])
    out["bmod"] = cols(i["b_mod_2"].reshape(-1)).reshape(P, DEPTH, -1)
    out["w2"] = i["a_cmp_w2"][0].reshape(2, 2, P, HD).transpose(2, 0, 1, 3).reshape(P, 2, 2, HD)
    out["posT"] = i["a_cmp_pos"][0].transpose(2, 0, 1)
    out["b1"] = i["a_cmp_b1"][0].reshape(2, 2, P).transpose(2, 0, 1)
    out["b2"] = np.broadcast_to(i["a_cmp_b2"][0][None], (P, 2, HD))
    out["gate_b"] = row(i["a_gate_b"][0])
    out["rope"] = out["rope"].reshape(P, TC, 2, 32)
    out["rope_cmp"] = out["rope_cmp"].reshape(P, 2, 32)
    out["cmp_bias"] = out["cmp_bias"].reshape(P, TC, N_CMP)
    out["cmp_seen"] = out["cmp_seen"].reshape(P, TC, N_CMP)
    out["sel"] = out["sel"][:NH].reshape(NH, 6, 2 * P)
    cw = [np.concatenate([i["conv_w"][l], i["conv_b"][l][None]], 0).reshape(4, 2 * FT, P).transpose(2, 0, 1)
          for l in range(DEPTH)]
    out["convw"] = np.stack(cw)
    out["w_route"] = np.stack([tiles(np.concatenate([i["moe_w_group_2"][l], i["moe_w_expert_2"][l]], 1))
                               .reshape(P, KT, G + E) for l in range(DEPTH)])
    out["b_group"] = np.stack([row(i["moe_b_group_2"][l]) for l in range(DEPTH)])
    out["b_expert"] = np.stack([row(i["moe_b_expert_2"][l]).reshape(P, G, EPG) for l in range(DEPTH)])
    out["first_final_g"] = row(i["final_norm"])
    out["final_g"] = row(i["final_norm_g_2"])
    return {n: np.ascontiguousarray(a) for n, a in out.items()}


def kernel(**inputs):
    import concourse.bacc as bacc
    from concourse.bass_utils import run_bass_kernel_spmd

    arrays = layout({n: np.asarray(a) for n, a in inputs.items()})
    nc = bacc.Bacc("TRN2", target_bir_lowering=False, num_devices=1)
    dram = {n: nc.dram_tensor("in_" + n, a.shape, mybir.dt.from_np(a.dtype), kind="ExternalInput").ap()
            for n, a in arrays.items()}
    out = nc.dram_tensor("out_x", (S, D), mybir.dt.float32, kind="ExternalOutput").ap()
    two_blocks(nc, dram, out)
    got = run_bass_kernel_spmd(nc, [{"in_" + n: a for n, a in arrays.items()}], core_ids=[0])
    return got.results[0]["out_x"].reshape(1, S, D)
```
